# Optimizing a Trainium2 kernel written in Bass

```python
import jax, jax.numpy as jnp
from jax import lax
import numpy as np

D_MODEL = 1024
BATCH = 1
SEQ = 512
DEPTH = 1
DEC_BATCH = 1
DEC_SEQ = 32
PAST_LEN = 256

CHUNK = 64
Q_BLOCK = 128
HEAD_DIM = 64
N_HEADS_A = 8
N_HEADS_B = 8
WIDTH_A = N_HEADS_A * HEAD_DIM
WIDTH_B = N_HEADS_B * HEAD_DIM
IDX_HEADS = 8
IDX_DIM = 64
TOPK_MAX = 256
ROPE_THETA = 500000.0
EPS = 1e-6
NEG_INF = -1e30
D_IN = 4 * WIDTH_A + IDX_HEADS * IDX_DIM + IDX_DIM + IDX_HEADS + 4 * WIDTH_B + 2 * D_MODEL

kernel_name = "dsa_stickbreaking_gated_hybrid_step"

def _split_points():
    sizes = [WIDTH_A] * 4 + [IDX_HEADS * IDX_DIM, IDX_DIM, IDX_HEADS] + [WIDTH_B] * 4 + [D_MODEL, D_MODEL]
    return [int(s) for s in np.cumsum(sizes)[:-1]]

def _rms_norm(x, g):
    xf = x.astype(jnp.float32)
    y = xf * lax.rsqrt(jnp.mean(xf * xf, axis=-1, keepdims=True) + EPS) * g.astype(jnp.float32)
    return y.astype(x.dtype)

def _rope(x, pos):
    rot = x.shape[-1] // 4
    half = rot // 2
    inv_freq = ROPE_THETA ** (-jnp.arange(half, dtype=jnp.float32) / half)
    ang = pos.astype(jnp.float32)[:, None] * inv_freq[None, :]
    cos = jnp.cos(ang)[:, None, :]
    sin = jnp.sin(ang)[:, None, :]
    xr = x[..., :rot].astype(jnp.float32)
    x1, x2 = xr[..., :half], xr[..., half:]
    rotated = jnp.concatenate([x1 * cos - x2 * sin, x2 * cos + x1 * sin], axis=-1).astype(x.dtype)
    return jnp.concatenate([rotated, x[..., rot:]], axis=-1)

def _project(x, pos, norm_g, w_in, q_norm_g, k_norm_g, idx_k_norm_g):
    B, T, _ = x.shape
    xn = _rms_norm(x, norm_g)
    h = jnp.einsum('btd,de->bte', xn, w_in)
    qa, ka, va, ua, qi, ki, wi, qb, kb, vb, ub, ga, gb = jnp.split(h, _split_points(), axis=-1)
    qa = _rope(_rms_norm(qa.reshape(B, T, N_HEADS_A, HEAD_DIM), q_norm_g), pos)
    ka = _rope(_rms_norm(ka.reshape(B, T, N_HEADS_A, HEAD_DIM), k_norm_g), pos)
    va = va.reshape(B, T, N_HEADS_A, HEAD_DIM)
    qi = _rope(qi.reshape(B, T, IDX_HEADS, IDX_DIM), pos)
    ki = _rope(_rms_norm(ki, idx_k_norm_g)[:, :, None, :], pos)[:, :, 0, :]
    wi = wi * (IDX_HEADS ** -0.5)
    qb = qb.reshape(B, T, N_HEADS_B, HEAD_DIM)
    kb = kb.reshape(B, T, N_HEADS_B, HEAD_DIM)
    vb = vb.reshape(B, T, N_HEADS_B, HEAD_DIM)
    return qa, ka, va, ua, qi, ki, wi, qb, kb, vb, ub, ga, gb

def _dsa_block(q, qi, wi, q_pos, k, v, ki, topk):
    S = k.shape[1]
    key_pos = jnp.arange(S, dtype=jnp.int32)
    limit = (q_pos // CHUNK + 1) * CHUNK
    admissible = key_pos[None, :] < limit[:, None]
    dots = jnp.einsum('bqhd,bsd->bqhs', qi.astype(jnp.float32), ki.astype(jnp.float32)) * (IDX_DIM ** -0.5)
    score = jnp.einsum('bqhs,bqh->bqs', jax.nn.relu(dots), wi.astype(jnp.float32))
    score = jnp.where(admissible[None], score, NEG_INF)
    _, idx = lax.top_k(score, topk)
    k_sel = jax.vmap(lambda kk, ii: kk[ii])(k, idx)
    v_sel = jax.vmap(lambda vv, ii: vv[ii])(v, idx)
    ok = idx < limit[None, :, None]
    logits = jnp.einsum('bqhd,bqkhd->bqhk', q.astype(jnp.float32), k_sel.astype(jnp.float32)) * (HEAD_DIM ** -0.5)
    logits = jnp.where(ok[:, :, None, :], logits, NEG_INF)
    p = jax.nn.softmax(logits, axis=-1)
    o = jnp.einsum('bqhk,bqkhd->bqhd', p, v_sel.astype(jnp.float32))
    return o.astype(q.dtype)

def _sb_block(q, q_pos, k, v):
    S = k.shape[1]
    key_pos = jnp.arange(S, dtype=jnp.int32)
    strict = (key_pos[None, :] < q_pos[:, None])[None, None]
    z = jnp.einsum('bqhd,bshd->bhqs', q.astype(jnp.float32), k.astype(jnp.float32)) * (HEAD_DIM ** -0.5)
    log1m = jnp.where(strict, jax.nn.log_sigmoid(-z), 0.0)
    after = lax.cumsum(log1m, axis=3, reverse=True) - log1m
    a = jnp.where(strict, jnp.exp(jax.nn.log_sigmoid(z) + after), 0.0)
    o = jnp.einsum('bhqs,bshd->bqhd', a, v.astype(jnp.float32))
    return o.astype(q.dtype)

def _sweep(fn, q_args, pos):
    B, T = q_args[0].shape[:2]
    nb = T // Q_BLOCK
    blk = lambda a: jnp.moveaxis(a.reshape(B, nb, Q_BLOCK, *a.shape[2:]), 1, 0)
    out = lax.map(lambda args: fn(*args), tuple(blk(a) for a in q_args) + (pos.reshape(nb, Q_BLOCK),))
    return jnp.moveaxis(out, 0, 1).reshape(B, T, *out.shape[3:])

def _layer(x, pos, past, topk, blocked, norm_g, w_in, q_norm_g, k_norm_g, idx_k_norm_g, w_a_out, w_b_out, w_o):
    B, T, _ = x.shape
    qa, ka, va, ua, qi, ki, wi, qb, kb, vb, ub, ga, gb = _project(x, pos, norm_g, w_in, q_norm_g, k_norm_g, idx_k_norm_g)
    new_rows = (ka, va, ki, kb, vb)
    if past is None:
        ka_all, va_all, ki_all, kb_all, vb_all = new_rows
    else:
        ka_all, va_all, ki_all, kb_all, vb_all = [jnp.concatenate([c.astype(n.dtype), n], axis=1) for c, n in zip(past, new_rows)]
    fa = lambda q_, qi_, wi_, p_: _dsa_block(q_, qi_, wi_, p_, ka_all, va_all, ki_all, topk)
    fb = lambda q_, p_: _sb_block(q_, p_, kb_all, vb_all)
    if blocked:
        oa = _sweep(fa, (qa, qi, wi), pos)
        ob = _sweep(fb, (qb,), pos)
    else:
        oa = fa(qa, qi, wi, pos)
        ob = fb(qb, pos)
    ya = jnp.einsum('bte,ed->btd', oa.reshape(B, T, WIDTH_A) * jax.nn.silu(ua), w_a_out)
    yb = jnp.einsum('bte,ed->btd', ob.reshape(B, T, WIDTH_B) * jax.nn.silu(ub), w_b_out)
    mixed = jax.nn.sigmoid(ga) * ya + jax.nn.sigmoid(gb) * yb
    y = x + jnp.einsum('btd,de->bte', mixed, w_o)
    return y, new_rows

def setup_inputs(seed: int = 0) -> dict:
    key = jax.random.key(seed)
    ks = jax.random.split(key, 16)
    nrm = lambda k, shape, scale: jax.random.normal(k, shape, jnp.float32) * scale
    return {
        "x_prompt": nrm(ks[0], (BATCH, SEQ, D_MODEL), 1.0),
        "x_sample": nrm(ks[1], (DEC_BATCH, DEC_SEQ, D_MODEL), 1.0),
        "cache_a_k": nrm(ks[2], (DEPTH, DEC_BATCH, PAST_LEN, N_HEADS_A, HEAD_DIM), 1.0),
        "cache_a_v": nrm(ks[3], (DEPTH, DEC_BATCH, PAST_LEN, N_HEADS_A, HEAD_DIM), 1.0),
        "cache_idx_k": nrm(ks[4], (DEPTH, DEC_BATCH, PAST_LEN, IDX_DIM), 1.0),
        "cache_b_k": nrm(ks[5], (DEPTH, DEC_BATCH, PAST_LEN, N_HEADS_B, HEAD_DIM), 1.0),
        "cache_b_v": nrm(ks[6], (DEPTH, DEC_BATCH, PAST_LEN, N_HEADS_B, HEAD_DIM), 1.0),
        "norm_g": 1.0 + nrm(ks[7], (DEPTH, D_MODEL), 0.02),
        "w_in": nrm(ks[8], (DEPTH, D_MODEL, D_IN), D_MODEL ** -0.5),
        "q_norm_g": 1.0 + nrm(ks[9], (DEPTH, HEAD_DIM), 0.02),
        "k_norm_g": 1.0 + nrm(ks[10], (DEPTH, HEAD_DIM), 0.02),
        "idx_k_norm_g": 1.0 + nrm(ks[11], (DEPTH, IDX_DIM), 0.02),
        "w_a_out": nrm(ks[12], (DEPTH, WIDTH_A, D_MODEL), WIDTH_A ** -0.5),
        "w_b_out": nrm(ks[13], (DEPTH, WIDTH_B, D_MODEL), WIDTH_B ** -0.5),
        "w_o": nrm(ks[14], (DEPTH, D_MODEL, D_MODEL), D_MODEL ** -0.5),
    }

def reference(x_prompt, x_sample, cache_a_k, cache_a_v, cache_idx_k, cache_b_k, cache_b_v,
              norm_g, w_in, q_norm_g, k_norm_g, idx_k_norm_g, w_a_out, w_b_out, w_o):
    seq = x_prompt.shape[1]
    past_len = cache_a_k.shape[2]
    dec_seq = x_sample.shape[1]
    pos_p = jnp.arange(seq, dtype=jnp.int32)
    pos_s = past_len + jnp.arange(dec_seq, dtype=jnp.int32)
    topk_p = min(TOPK_MAX, seq // 4)
    topk_s = min(TOPK_MAX, (past_len + dec_seq) // 4)
    yp, ys = x_prompt, x_sample
    new_p, new_s = [], []
    for l in range(DEPTH):
        params = (norm_g[l], w_in[l], q_norm_g[l], k_norm_g[l], idx_k_norm_g[l], w_a_out[l], w_b_out[l], w_o[l])
        yp, rows_p = _layer(yp, pos_p, None, topk_p, True, *params)
        past = (cache_a_k[l], cache_a_v[l], cache_idx_k[l], cache_b_k[l], cache_b_v[l])
        ys, rows_s = _layer(ys, pos_s, past, topk_s, False, *params)
        new_p.append(rows_p)
        new_s.append(rows_s)
    stk = lambda rows, i: jnp.stack([r[i] for r in rows], axis=0)
    return (yp, ys,
            stk(new_p, 0), stk(new_p, 1), stk(new_p, 2), stk(new_p, 3), stk(new_p, 4),
            stk(new_s, 0), stk(new_s, 1), stk(new_s, 2), stk(new_s, 3), stk(new_s, 4))


_drawn_inputs = setup_inputs


def setup_inputs(seed=0):
    import zlib

    import numpy as np

    out = dict(_drawn_inputs(seed))
    spreads = {}
    factors = {'cache_b_k': 3.033, 'norm_g': 2.844, 'q_norm_g': 8.0, 'idx_k_norm_g': 2.759}
    for name, (base, spread) in spreads.items():
        noise = np.random.default_rng([zlib.crc32(name.encode()), seed]).standard_normal(out[name].shape)
        drawn = base * np.exp(spread * noise) if base else spread * noise
        out[name] = __import__('jax').numpy.asarray(drawn.astype(out[name].dtype))
    for name, factor in factors.items():
        out[name] = (out[name] * factor).astype(out[name].dtype)
    return out
```

```python
from contextlib import ExitStack

import numpy as np

import concourse.bass as bass
from concourse import mybir

F32 = mybir.dt.float32
F32R = mybir.dt.float32r
ALU = mybir.AluOpType
ACT = mybir.ActivationFunctionType
AX = mybir.AxisListType

P = 128
D = 1024
KC = D // P
SEQ, DEC, PAST = 512, 32, 256
NT = SEQ + DEC
HALF_NT = NT // 2
H, HD = 8, 64
PAIRS = H // 2
W = H * HD
EC = W // P
CHUNK = 64
TOPK_P = min(256, SEQ // 4)
TOPK_S = min(256, (PAST + DEC) // 4)
SKEYS = PAST + DEC
KEYS = SEQ + SKEYS
EPS = 1e-6
NEG = -1e30
TAKEN = -3e38
ROT = HD // 4
HR = ROT // 2
UC = 256
TILES = [(0, P), (P, P), (2 * P, P), (3 * P, P), (SEQ, DEC)]

QA, KA, VA, UA, QI = (W * i for i in range(5))
KI = QI + W
WI = KI + HD
QB = WI + H
KB, VB, UB = QB + W, QB + 2 * W, QB + 3 * W
GA = QB + 4 * W
GB = GA + D
KW = HD + H

QOFF = {3: 0, 2: 512, 0: 896, 1: 1024}
KOFF = {0: 0, 1: 512, 3: 896, 2: 1024}
PACK = 1280

UNITS = [("kw", "kw"), ("qi0", "tm"), ("qi1", "tm"), ("vb0", "tm"), ("vb1", "tm"), ("kb0", "tm"),
         ("kb1", "tm"), ("qb0", "fm"), ("qb1", "fm"), ("ka0", "tm"), ("ka1", "tm"), ("qa0", "tm"),
         ("qa1", "tm"), ("va0", "tm"), ("va1", "tm"), ("ua0", "fm"), ("ua1", "fm"), ("ub0", "fm"),
         ("ub1", "fm")]
COL = {"kw": KI, "qi": QI, "vb": VB, "kb": KB, "qb": QB, "ka": KA, "qa": QA, "va": VA, "ua": UA, "ub": UB}
U = {name: i for i, (name, _) in enumerate(UNITS)}
N_PROJ = len(UNITS)
for _d in range(D // P):
    UNITS += [(f"gate{_d}", "gate"), (f"mix{_d}", "mix")]
UNITS += [(f"out{_o}", "out") for _o in range(D // UC)]

GROUPS = []
FIRST_GROUP, LAST_GROUP = {}, {}
for _u in range(N_PROJ):
    _kind = UNITS[_u][1]
    FIRST_GROUP[_u] = len(GROUPS)
    if _kind == "tm":
        GROUPS += [(_u, t) for t in range(5)]
    elif _kind == "kw":
        GROUPS += [(_u, (0, h)) for h in range(2)]
    else:
        GROUPS += [(_u, (f, h)) for f in range(UC // P) for h in range(2)]
    LAST_GROUP[_u] = len(GROUPS) - 1
BANK = []
for _g, (_u, _) in enumerate(GROUPS):
    _busy = U["ka0"] <= _u <= U["qa1"] or _u >= U["ua0"]
    BANK.append(7 if _busy or _g % 2 else 6)


def unit_cols(u):
    kind = UNITS[u][1]
    return KC * KW if kind == "kw" else 2 * EC * P if kind == "mix" else KC * UC


def raw_count(u):
    return sum(32 if UNITS[v][1] in ("gate", "mix") else 16 for v in range(u % 2, u + 1, 2))


def group_evacuated_before(g):
    for p in range(g - 1, -1, -1):
        if BANK[p] == BANK[g]:
            return p + 1
    return 0


ITEMS = ([("iq", p) for p in range(PAIRS)] + [("iqs", 0), ("ik", 0), ("ikx", 0)]
         + [("bk", p) for p in range(PAIRS)] + [("bkx", p) for p in range(PAIRS)]
         + [("ak", p) for p in range(PAIRS)] + [("akx", p) for p in range(PAIRS)]
         + [("aq", p) for p in range(PAIRS)] + [("aqs", 0)])
I_ITEMS = range(0, 7)
B_ITEMS = range(7, 15)
A_ITEMS = range(15, 28)
ITEM_BANKS = 6


def by_act(n):
    return (n + 1) // 2


def by_dve(n):
    return n // 2


SCORED = [3, 2, 1, "s"]
DOTS = [(h, b) for h in range(H) for b in SCORED]
ROUNDS = {3: TOPK_P // 8, 2: TOPK_P // 8, 1: TOPK_P // 8, "s": TOPK_S // 8}


def n_keys(b):
    return SKEYS if b == "s" else P * (b + 1)


def build(nc, x_prompt, x_sample, cache_a_k, cache_a_v, cache_idx_k, cache_b_k, cache_b_v, norm_g, w_in,
          q_norm_g, k_norm_g, idx_k_norm_g, w_a_out, w_b_out, w_o, rope_const,
          y_prompt, y_sample, new_a_k_p, new_a_v_p, new_idx_k_p, new_b_k_p, new_b_v_p,
          new_a_k_s, new_a_v_s, new_idx_k_s, new_b_k_s, new_b_v_s):
    with ExitStack() as ctx:
        place = [(nc.sbuf_base + 63) // 64 * 64]

        def sb_at(name, cols, dt, at):
            return nc.alloc_sbuf_tensor_at(name, [P, cols], dt, offset=at)

        def sb(name, cols, dt=F32):
            at = place[0]
            place[0] += (4 * cols + 31) // 32 * 32
            return sb_at(name, cols, dt, at)

        def sem(name):
            return ctx.enter_context(nc.semaphore(name))

        xhi = sb("xhi", KC * NT, F32R)[:, :].rearrange("p (c n) -> p c n", c=KC)
        xlo = sb("xlo", KC * NT, F32R)[:, :].rearrange("p (c n) -> p c n", c=KC)
        raw = sb("raw", 2 * KC * UC)[:, :].rearrange("p (s n) -> p s n", s=2)
        whi = sb("whi", 2 * KC * UC, F32R)[:, :].rearrange("p (s n) -> p s n", s=2)
        wlo = sb("wlo", 2 * KC * UC, F32R)[:, :].rearrange("p (s n) -> p s n", s=2)
        at_v = place[0]
        vals = sb("vals", 7 * W)[:, :].rearrange("p (t n) -> p t n", t=7)
        q_flat = sb("q_flat", H * NT)[:, :]
        qT = q_flat[:, 0:H * SEQ].rearrange("p (h n) -> p h n", h=H)
        qS = q_flat[:, H * SEQ:H * NT].rearrange("p (h n) -> p h n", h=H)
        kT = sb("kT", PAIRS * KEYS)[:, :].rearrange("p (c n) -> p c n", c=PAIRS)
        at_tm = place[0]
        tm = sb("tm", 5 * D)[:, :].rearrange("p (t n) -> p t n", t=5)
        wk = sb("wk", 5 * PACK)[:, :].rearrange("p (s n) -> p s n", s=5)
        oT = sb("oT", 2 * PAIRS * NT)[:, :].rearrange("p (c n) -> p c n", c=2 * PAIRS)
        bias = sb("bias", PACK)[:, :]
        bias_s = sb("bias_s", SKEYS)[:, :]
        bias_r = sb("bias_r", SKEYS)[:, :]
        square = sb("square", W)[:, :]
        rot = sb("rot", 2 * 4 * 9 * ROT)[:, :].rearrange("p (a n) -> p a n", a=2)
        ident = sb("ident", P)[:, :]
        tri = sb("tri", P)[:, :]
        ones = sb("ones", P)[:, :]
        rope = sb("rope", 5 * 32)[:, :].rearrange("p (t n) -> p t n", t=5)
        gk = sb("gk", 3 * HD)[:, :].rearrange("p (a n) -> p a n", a=3)
        gx = sb("gx", KC)[:, :]
        xss = sb("xss", 8)[:, :]
        xrs = sb("xrs", 8)[:, :]
        half = sb("half", 5 * H)[:, :]
        nss = sb("nss", 5 * H)[:, :].rearrange("p (t h) -> p t h", t=5)
        nrs = sb("nrs", 5 * H)[:, :].rearrange("p (t h) -> p t h", t=5)
        wis = sb("wis", 5 * H)[:, :].rearrange("p (t h) -> p t h", t=5)
        top = sb("top", 4 * 8)[:, :].rearrange("p (b n) -> p b n", b=4)
        mx = sb("mx", 8)[:, :]
        nmx = sb("nmx", 8)[:, :]
        esum = sb("esum", 8)[:, :]
        rsum = sb("rsum", 8)[:, :]
        assert place[0] <= nc.sbuf_usable_end
        ohi = sb_at("ohi", 2 * PAIRS * NT, F32R, at_v)[:, :].rearrange("p (c n) -> p c n", c=2 * PAIRS)
        olo = sb_at("olo", 2 * PAIRS * NT, F32R, at_v + 8 * PAIRS * NT)[:, :].rearrange("p (c n) -> p c n", c=2 * PAIRS)
        assert at_v + 16 * PAIRS * NT <= at_tm
        res = sb_at("res", 5 * D, F32, at_v)[:, :].rearrange("p (t n) -> p t n", t=5)
        u = tm.rearrange("p t n -> p (t n)")[:, 0:H * NT].rearrange("p (c n) -> p c n", c=H)
        mhi = sb_at("mhi", KC * NT, F32R, at_tm)[:, :].rearrange("p (c n) -> p c n", c=KC)
        mlo = sb_at("mlo", KC * NT, F32R, at_tm + 4 * KC * NT)[:, :].rearrange("p (c n) -> p c n", c=KC)
        sg = oT
        sgu = wk.rearrange("p s n -> p (s n)")[:, 0:H * NT].rearrange("p (c n) -> p c n", c=H)

        PS = ctx.enter_context(nc.psum_tensor("PS", [P, 8 * 512], F32))
        ps = PS[:, :].rearrange("p (b n) -> p b n", b=8)
        flat = PS[:, :]

        x_in = [sem(f"x_in{t}") for t in range(5)]
        const_in = sem("const_in")
        cache_i_in = sem("cache_i_in")
        cache_bk_in = sem("cache_bk_in")
        cache_bv_in = sem("cache_bv_in")
        cache_ak_in = sem("cache_ak_in")
        cache_av_in = sem("cache_av_in")
        res_in = sem("res_in")
        raw_ready = [sem("raw_ready0"), sem("raw_ready1")]
        w_hi = sem("w_hi")
        w_lo = sem("w_lo")
        const_ready = sem("const_ready")
        x_sq = sem("x_sq")
        x_rs = sem("x_rs")
        x_scaled = sem("x_scaled")
        x_tr = sem("x_tr")
        x_g = sem("x_g")
        x_hi = sem("x_hi")
        x_lo = sem("x_lo")
        group_done = sem("group_done")
        group_out = sem("group_out")
        kw_tr = sem("kw_tr")
        kw_out = sem("kw_out")
        ki_ss = sem("ki_ss")
        ki_rs = sem("ki_rs")
        i_rows = sem("i_rows")
        item_done = sem("item_done")
        item_act = sem("item_act")
        item_dve = sem("item_dve")
        dot_done = sem("dot_done")
        relu_done = sem("relu_done")
        acc_done = sem("acc_done")
        topk_step = sem("topk_step")
        bias_done = sem("bias_done")
        bias_rep = sem("bias_rep")
        nk_ss, nk_rs, nk_r, nk_g, k_rows = (sem(n) for n in ("nk_ss", "nk_rs", "nk_r", "nk_g", "k_rows"))
        nq_ss, nq_rs, nq_r, nq_g, q_rows = (sem(n) for n in ("nq_ss", "nq_rs", "nq_r", "nq_g", "q_rows"))
        z_done, t_done, l_done, lm_done, c_done, a_done, am_done, pv_done, pv_out = (
            sem(n) for n in ("z_done", "t_done", "l_done", "lm_done", "c_done", "a_done", "am_done", "pv_done", "pv_out"))
        lg_done, mx_done, e_done, p_done, pt_done, pt_out, av_done, av_out = (
            sem(n) for n in ("lg_done", "mx_done", "e_done", "p_done", "pt_done", "pt_out", "av_done", "av_out"))
        u_sig, ou_done, os_done, o_hi, o_lo = (sem(n) for n in ("u_sig", "ou_done", "os_done", "o_hi", "o_lo"))
        gates_done, gates_sig, mix_done, mix_used, mixed, m_hi, m_lo = (
            sem(n) for n in ("gates_done", "gates_sig", "mix_done", "mix_used", "mixed", "m_hi", "m_lo"))
        y_done, y_out = sem("y_done"), sem("y_out")
        st_ki, st_kb, st_vb, st_ka, st_va, st_y = (sem(n) for n in ("st_ki", "st_kb", "st_vb", "st_ka", "st_va", "st_y"))
        act_chain, dve_chain, pool_chain = sem("act_chain"), sem("dve_chain"), sem("pool_chain")

        def wview(buf, uu):
            return buf[:, uu % 2, 0:unit_cols(uu)].rearrange(
                "p (c n) -> p c n", c=2 * EC if UNITS[uu][1] == "mix" else KC)

        def rows_p(ap):
            ap = ap.rearrange("a b s h d -> (a b s) (h d)") if len(ap.shape) == 5 else ap.rearrange("a b s d -> (a b s) d")
            return ap.rearrange("(t p) n -> p t n", p=P)

        def rows_s(ap):
            return ap.rearrange("a b s h d -> (a b s) (h d)") if len(ap.shape) == 5 else ap.rearrange("a b s d -> (a b s) d")

        def cached(ap):
            return rows_p(ap)

        xp = x_prompt.rearrange("b (t p) d -> p (b t) d", p=P)
        xs = x_sample.rearrange("b s d -> (b s) d")
        wi_v = w_in.rearrange("l (c p) e -> p (l c) e", p=P)
        wa_v = w_a_out.rearrange("l (c p) e -> p (l c) e", p=P)
        wb_v = w_b_out.rearrange("l (c p) e -> p (l c) e", p=P)
        wo_v = w_o.rearrange("l (c p) e -> p (l c) e", p=P)
        cstage_i = wk[:, 4, 0:256].rearrange("p (t n) -> p t n", t=2)
        cstage_b = wk[:, 4, 256:1280].rearrange("p (t n) -> p t n", t=2)
        cstage_a = cstage_b

        block = ctx.enter_context(nc.Block())

        @block.sync
        def _(sp):
            for t in range(4):
                sp.dma_start(tm[:, t, :], xp[:, t, :]).then_inc(x_in[t], 16)
            sp.dma_start(tm[0:DEC, 4, :], xs).then_inc(x_in[4], 16)
            sp.dma_start(gx, norm_g).then_inc(const_in, 16)
            sp.dma_start(rope, rope_const).then_inc(const_in, 16)
            sp.dma_start(gk[:, 0, :], q_norm_g).then_inc(const_in, 16)
            sp.dma_start(gk[:, 1, :], k_norm_g).then_inc(const_in, 16)
            sp.dma_start(gk[:, 2, :], idx_k_norm_g).then_inc(const_in, 16)

            def load_unit(uu):
                if uu >= 2:
                    sp.wait_ge(w_lo, uu - 1)
                name, kind = UNITS[uu]
                dst, ready = wview(raw, uu), raw_ready[uu % 2]
                if kind in ("tm", "fm"):
                    c = COL[name[:2]] + UC * int(name[2])
                    sp.dma_start(dst, wi_v[:, :, c:c + UC]).then_inc(ready, 16)
                elif kind == "kw":
                    sp.dma_start(dst, wi_v[:, :, KI:KI + KW]).then_inc(ready, 16)
                elif kind == "gate":
                    c = P * int(name[4:])
                    sp.dma_start(dst[:, :, 0:P], wi_v[:, :, GA + c:GA + c + P]).then_inc(ready, 16)
                    sp.dma_start(dst[:, :, P:UC], wi_v[:, :, GB + c:GB + c + P]).then_inc(ready, 16)
                elif kind == "mix":
                    c = P * int(name[3:])
                    sp.dma_start(dst[:, 0:EC, :], wa_v[:, :, c:c + P]).then_inc(ready, 16)
                    sp.dma_start(dst[:, EC:2 * EC, :], wb_v[:, :, c:c + P]).then_inc(ready, 16)
                else:
                    c = UC * int(name[3:])
                    sp.dma_start(dst, wo_v[:, :, c:c + UC]).then_inc(ready, 16)

            for uu in range(0, 3):
                load_unit(uu)
            sp.wait_ge(x_lo, 5)
            for c in range(2):
                sp.dma_start(cstage_i[:, :, HD * c:HD * c + HD], cached(cache_idx_k)).then_inc(cache_i_in, 16)
            sp.dma_start(cstage_b, cached(cache_b_k)).then_inc(cache_bk_in, 16)
            sp.dma_start(vals[:, 4:6, :], cached(cache_b_v)).then_inc(cache_bv_in, 16)
            for uu in range(3, U["kb0"] + 1):
                load_unit(uu)
            sp.wait_ge(i_rows, 1)
            sp.dma_start(rows_p(new_idx_k_p), tm[:, 0:4, W:W + HD]).then_inc(st_ki, 16)
            sp.dma_start(rows_s(new_idx_k_s), tm[0:DEC, 4, W:W + HD]).then_inc(st_ki, 16)
            load_unit(U["kb1"])
            sp.wait_ge(group_out, LAST_GROUP[U["vb1"]] + 1)
            sp.dma_start(rows_p(new_b_v_p), vals[:, 0:4, :]).then_inc(st_vb, 16)
            sp.dma_start(rows_s(new_b_v_s), vals[0:DEC, 6, :]).then_inc(st_vb, 16)
            load_unit(U["qb0"])
            load_unit(U["qb1"])
            sp.wait_ge(group_out, LAST_GROUP[U["kb1"]] + 1)
            sp.dma_start(rows_p(new_b_k_p), tm[:, 0:4, 0:W]).then_inc(st_kb, 16)
            sp.dma_start(rows_s(new_b_k_s), tm[0:DEC, 4, 0:W]).then_inc(st_kb, 16)
            for uu in range(U["ka0"], U["va1"] + 1):
                load_unit(uu)
            sp.wait_ge(bias_done, 1)
            for r in range(4):
                sp.dma_start(bias_r[32 * r:32 * r + 32, :], bias_s[0:DEC, :]).then_inc(bias_rep, 16)
            sp.wait_ge(pv_done, 9)
            sp.dma_start(cstage_a, cached(cache_a_k)).then_inc(cache_ak_in, 16)
            sp.dma_start(vals[:, 4:6, :], cached(cache_a_v)).then_inc(cache_av_in, 16)
            load_unit(U["ua0"])
            sp.wait_ge(k_rows, 1)
            sp.dma_start(rows_p(new_a_k_p), tm[:, 0:4, W:2 * W]).then_inc(st_ka, 16)
            sp.dma_start(rows_s(new_a_k_s), tm[0:DEC, 4, W:2 * W]).then_inc(st_ka, 16)
            load_unit(U["ua1"])
            sp.wait_ge(group_out, LAST_GROUP[U["va1"]] + 1)
            sp.dma_start(rows_p(new_a_v_p), vals[:, 0:4, :]).then_inc(st_va, 16)
            sp.dma_start(rows_s(new_a_v_s), vals[0:DEC, 6, :]).then_inc(st_va, 16)
            for uu in range(U["ub0"], len(UNITS)):
                load_unit(uu)
                if UNITS[uu][0] == "out1":
                    sp.wait_ge(mix_done, D // P)
                    sp.dma_start(res[:, 0:4, :], xp).then_inc(res_in, 16)
                    sp.dma_start(res[0:DEC, 4, :], xs).then_inc(res_in, 16)
            yp = y_prompt.rearrange("b (t p) d -> p (b t) d", p=P)
            ys = y_sample.rearrange("b s d -> (b s) d")
            for g in range(20):
                o, t = divmod(g, 5)
                sp.wait_ge(y_out, g + 1)
                dst, n = (yp[:, t, :], P) if t < 4 else (ys, DEC)
                sp.dma_start(dst[:, UC * o:UC * o + UC], res[0:n, t, UC * o:UC * o + UC]).then_inc(st_y, 16)
            sp.wait_ge(st_y, 16 * 20)
            for s in (st_ki, st_kb, st_vb, st_ka, st_va):
                sp.wait_ge(s, 32)

        @block.tensor
        def _(pe):
            PASSES = ((0, 0), (0, 1), (1, 0))
            xpart, wpart = (xhi, xlo), (whi, wlo)

            pe.wait_ge(const_ready, 4)
            for t, (t0, n) in enumerate(TILES):
                pe.wait_ge(x_scaled, t + 1)
                if t >= 2:
                    pe.wait_ge(x_g, t - 1)
                for c in range(KC):
                    col = 1024 * (t % 2) + P * c
                    last = pe.transpose(flat[:, col:col + n], tm[0:n, t, P * c:P * c + P], ident[0:n, 0:n])
                last.then_inc(x_tr, 1)
            pe.wait_ge(x_lo, 5)

            def group(g):
                uu, part = GROUPS[g]
                if g == FIRST_GROUP[uu]:
                    pe.wait_ge(w_lo, uu + 1)
                if group_evacuated_before(g):
                    pe.wait_ge(group_out, group_evacuated_before(g))
                bank = ps[:, BANK[g], :]
                k = 0
                for c in range(KC):
                    for a, b in PASSES:
                        w = wview(wpart[b], uu)[:, c, :]
                        if UNITS[uu][1] == "tm":
                            t0, n = TILES[part]
                            out, lhsT, rhs = bank[0:n, 0:UC], xpart[a][:, c, t0:t0 + n], w
                        else:
                            f, h = part
                            m = KW if UNITS[uu][1] == "kw" else P
                            out, lhsT = bank[0:m, 0:HALF_NT], w[:, P * f:P * f + m]
                            rhs = xpart[a][:, c, HALF_NT * h:HALF_NT * (h + 1)]
                        mm = pe.matmul(out, lhsT, rhs, start=(k == 0), stop=(k == 23))
                        k += 1
                mm.then_inc(group_done, 1)

            def unit(name):
                for g in range(FIRST_GROUP[U[name]], LAST_GROUP[U[name]] + 1):
                    group(g)

            unit("kw")
            group(FIRST_GROUP[U["qi0"]])
            pe.wait_ge(group_out, LAST_GROUP[U["kw"]] + 1)
            for t, (t0, n) in enumerate(TILES):
                last = pe.transpose(ps[0:n, 5, KW * t:KW * t + KW], wk[0:KW, 3, t0:t0 + n], ident[0:KW, 0:KW])
            last.then_inc(kw_tr, 1)
            for g in range(FIRST_GROUP[U["qi0"]] + 1, LAST_GROUP[U["qi0"]] + 1):
                group(g)
            unit("qi1")
            unit("vb0")

            def item(n):
                kind, p = ITEMS[n]
                if n >= ITEM_BANKS:
                    m = n - ITEM_BANKS + 1
                    if (m - 1) % 2 == 0:
                        pe.wait_ge(item_act, by_act(m))
                    else:
                        pe.wait_ge(item_dve, by_dve(m))
                bank = ps[:, n % ITEM_BANKS, :]
                src = {"ik": 5 * P, "bk": P * p, "ak": W + P * p, "iq": P * p, "aq": P * p}
                if kind in src:
                    for t in range(4):
                        last = pe.transpose(bank[:, P * t:P * t + P], tm[:, t, src[kind]:src[kind] + P], ident)
                elif kind in ("iqs", "aqs"):
                    for q in range(PAIRS):
                        last = pe.transpose(bank[:, DEC * q:DEC * q + DEC], tm[0:DEC, 4, P * q:P * q + P],
                                            ident[0:DEC, 0:DEC])
                else:
                    s = src[kind[:2]]
                    stage = {"ikx": cstage_i, "bkx": cstage_b, "akx": cstage_a}[kind]
                    c = 0 if kind == "ikx" else P * p
                    for t in range(2):
                        pe.transpose(bank[:, P * t:P * t + P], stage[:, t, c:c + P], ident)
                    last = pe.transpose(bank[:, PAST:SKEYS], tm[0:DEC, 4, s:s + P], ident[0:DEC, 0:DEC])
                last.then_inc(item_done, 1)

            pe.wait_ge(i_rows, 1)
            pe.wait_ge(cache_i_in, 32)
            for n in I_ITEMS:
                item(n)
            unit("vb1")
            pe.wait_ge(item_act, by_act(I_ITEMS.stop))
            pe.wait_ge(item_dve, by_dve(I_ITEMS.stop))
            for n, (h, b) in enumerate(DOTS):
                if n >= 6:
                    pe.wait_ge(relu_done, n - 5)
                m, q, k0 = (DEC, qS[:, h, :], SEQ) if b == "s" else (P, qT[:, h, P * b:P * b + P], 0)
                pe.matmul(ps[0:m, n % 6, 0:n_keys(b)], q, kT[:, 0, k0:k0 + n_keys(b)],
                          start=True, stop=True).then_inc(dot_done, 1)
            unit("kb0")
            unit("kb1")
            unit("qb0")
            pe.wait_ge(relu_done, len(DOTS))
            pe.wait_ge(cache_bk_in, 16)
            for n in B_ITEMS:
                item(n)
            unit("qb1")
            pe.wait_ge(group_out, LAST_GROUP[U["qb1"]] + 1)
            pe.wait_ge(item_act, by_act(B_ITEMS.stop))
            pe.wait_ge(item_dve, by_dve(B_ITEMS.stop))
            pe.wait_ge(cache_bv_in, 16)

            def z(s):
                if s >= 2:
                    pe.wait_ge(a_done, s - 1)
                base = 1536 * (s % 2)
                if s < H:
                    for j in (0, 1, 3, 2):
                        nq = SEQ - P * j
                        o = base + KOFF[j]
                        last = pe.matmul(flat[:, o:o + nq], kT[:, s // 2, P * j:P * j + P], qT[:, s, P * j:SEQ],
                                         start=(j != 3), stop=True, skip_group_check=True)
                else:
                    for b in range(3):
                        kn = P if b < 2 else DEC
                        for p in range(PAIRS):
                            o = base + 256 * b + 64 * p
                            last = pe.matmul(flat[0:kn, o:o + 64], kT[:, p, SEQ + P * b:SEQ + P * b + kn],
                                             q_flat[:, H * SEQ + 64 * p:H * SEQ + 64 * p + 64],
                                             start=(p == 0 and b != 1), stop=True,
                                             skip_group_check=True)
                last.then_inc(z_done, 1)

            def cumulate(s):
                pe.wait_ge(lm_done, s + 1)
                base = 1536 * (s % 2)
                L = wk[:, 1 + s % 2, :]
                if s < H:
                    for j in range(4):
                        nq = SEQ - P * j
                        last = pe.matmul(flat[:, base + KOFF[j]:base + KOFF[j] + nq], tri, L[:, KOFF[j]:KOFF[j] + nq],
                                         start=False, stop=True, skip_group_check=True)
                        for j2 in range(j + 1, 4):
                            n2 = SEQ - P * j2
                            o = base + KOFF[j] + P * (j2 - j)
                            last = pe.matmul(flat[:, o:o + n2], ones, L[:, KOFF[j2]:KOFF[j2] + n2],
                                             start=False, stop=True, skip_group_check=True)
                else:
                    for b in range(3):
                        kn = P if b < 2 else DEC
                        o = base + 256 * b
                        last = pe.matmul(flat[0:kn, o:o + 256], tri[0:kn, 0:kn], L[0:kn, 256 * b:256 * b + 256],
                                         start=False, stop=True, skip_group_check=True)
                        for b2 in range(b + 1, 3):
                            k2 = P if b2 < 2 else DEC
                            last = pe.matmul(flat[0:kn, o:o + 256], ones[0:k2, 0:kn], L[0:k2, 256 * b2:256 * b2 + 256],
                                             start=False, stop=True, skip_group_check=True)
                last.then_inc(c_done, 1)

            def weigh(s, probs, ready, out_ready, done, sample_col):
                pe.wait_ge(ready, s + 1)
                if s % 2 == 0 and s >= 2:
                    pe.wait_ge(out_ready, s // 2)
                if s < H:
                    r = HD * (s % 2)
                    for j in range(4):
                        last = pe.matmul(ps[r:r + HD, 6, P * j:SEQ], vals[:, j, HD * s:HD * s + HD],
                                         probs[:, KOFF[j]:KOFF[j] + SEQ - P * j], start=(j == 0), stop=(j == 3),
                                         skip_group_check=True)
                else:
                    for h in range(H):
                        r = HD * (h % 2)
                        for b in range(3):
                            kn = P if b < 2 else DEC
                            c = sample_col(h, b)
                            last = pe.matmul(ps[r:r + HD, 6, DEC * (h // 2):DEC * (h // 2) + DEC],
                                             vals[0:kn, 4 + b, HD * h:HD * h + HD], probs[0:kn, c:c + DEC],
                                             start=(b == 0), stop=(b == 2), skip_group_check=True)
                last.then_inc(done, 1)

            g = FIRST_GROUP[U["ka0"]]
            for s in range(11):
                for part in range(2):
                    if g <= LAST_GROUP[U["qa1"]]:
                        group(g)
                        g += 1
                    if part == 0 and s < 9:
                        z(s)
                if 1 <= s <= 9:
                    cumulate(s - 1)
                if s >= 2:
                    weigh(s - 2, wk[:, 3 + s % 2, :], am_done, pv_out, pv_done, lambda h, b: 256 * b + DEC * h)
            pe.wait_ge(pv_out, 5)
            unit("va0")
            unit("va1")

            pe.wait_ge(k_rows, 1)
            pe.wait_ge(cache_ak_in, 16)
            for n in A_ITEMS:
                if ITEMS[n] == ("aq", 0):
                    pe.wait_ge(q_rows, 1)
                item(n)
            pe.wait_ge(item_act, by_act(A_ITEMS.stop))
            pe.wait_ge(item_dve, by_dve(A_ITEMS.stop))
            pe.wait_ge(group_out, LAST_GROUP[U["va1"]] + 1)
            pe.wait_ge(cache_av_in, 16)

            def logits(s):
                if s >= 1:
                    pe.wait_ge(mx_done, s)
                if s < H:
                    for i in (3, 2, 0, 1):
                        last = pe.matmul(flat[:, QOFF[i]:QOFF[i] + n_keys(i)], qT[:, s, P * i:P * i + P],
                                         kT[:, s // 2, 0:n_keys(i)], start=True, stop=True, skip_group_check=True)
                else:
                    for p in range(PAIRS):
                        r = HD * (p % 2)
                        last = pe.matmul(ps[r:r + HD, p // 2, 0:SKEYS], q_flat[:, H * SEQ + 64 * p:H * SEQ + 64 * p + 64],
                                         kT[:, p, SEQ:KEYS], start=True, stop=True)
                last.then_inc(lg_done, 1)

            def turn(s):
                pe.wait_ge(p_done, s + 1)
                if s >= 1:
                    pe.wait_ge(pt_out, s)
                pr = wk[:, s % 2, :]
                if s < H:
                    for i in range(4):
                        for j in range(i + 1):
                            o = 1536 + KOFF[j] + P * (i - j)
                            last = pe.transpose(flat[:, o:o + P], pr[:, QOFF[i] + P * j:QOFF[i] + P * j + P], ident)
                else:
                    for q in range(2):
                        for b in range(3):
                            kn = P if b < 2 else DEC
                            last = pe.transpose(ps[0:kn, 3 + q, P * b:P * b + P],
                                                pr[:, 512 * q + P * b:512 * q + P * b + kn], ident)
                last.then_inc(pt_done, 1)

            g = FIRST_GROUP[U["ua0"]]
            for s in range(11):
                if s < 9:
                    logits(s)
                if s < H:
                    group(g)
                    g += 1
                if 1 <= s <= 9:
                    turn(s - 1)
                if s < H:
                    group(g)
                    g += 1
                if s >= 2:
                    weigh(s - 2, wk[:, 2 + s % 2, :], pt_out, av_out, av_done,
                          lambda h, b: 512 * (h // 4) + P * b + DEC * (h % 4))

            pe.wait_ge(group_out, len(GROUPS))
            pe.wait_ge(av_out, 5)
            opart = (ohi, olo)
            for d in range(D // P):
                uu = N_PROJ + 2 * d
                pe.wait_ge(w_lo, uu + 1)
                if d >= 1:
                    pe.wait_ge(gates_sig, d)
                for f in range(2):
                    for h in range(2):
                        k = 0
                        for c in range(KC):
                            for a, b in PASSES:
                                mm = pe.matmul(ps[:, 2 * f + h, 0:HALF_NT], wview(wpart[b], uu)[:, c, P * f:P * f + P],
                                               xpart[a][:, c, HALF_NT * h:HALF_NT * (h + 1)], start=(k == 0), stop=(k == 23))
                                k += 1
                mm.then_inc(gates_done, 1)
                uu += 1
                if d == 0:
                    pe.wait_ge(o_lo, 4)
                pe.wait_ge(w_lo, uu + 1)
                if d >= 1:
                    pe.wait_ge(mix_used, d)
                for br in range(2):
                    for h in range(2):
                        k = 0
                        for c in range(EC):
                            for a, b in PASSES:
                                mm = pe.matmul(ps[:, 4 + 2 * br + h, 0:HALF_NT], wview(wpart[b], uu)[:, EC * br + c, :],
                                               opart[a][:, EC * br + c, HALF_NT * h:HALF_NT * (h + 1)],
                                               start=(k == 0), stop=(k == 11))
                                k += 1
                mm.then_inc(mix_done, 1)

            pe.wait_ge(m_lo, D // P)
            pe.wait_ge(mix_used, D // P)
            mpart = (mhi, mlo)
            for g in range(20):
                o, t = divmod(g, 5)
                uu = N_PROJ + 2 * (D // P) + o
                if t == 0:
                    pe.wait_ge(w_lo, uu + 1)
                if g >= 8:
                    pe.wait_ge(y_out, g - 7)
                t0, n = TILES[t]
                k = 0
                for c in range(KC):
                    for a, b in PASSES:
                        mm = pe.matmul(ps[0:n, g % 8, 0:UC], mpart[a][:, c, t0:t0 + n], wview(wpart[b], uu)[:, c, :],
                                       start=(k == 0), stop=(k == 23))
                        k += 1
                mm.then_inc(y_done, 1)

        @block.scalar
        def _(act):
            chain = [0]

            def link(ins):
                chain[0] += 1
                ins.then_inc(act_chain, 1)
                act.wait_ge(act_chain, chain[0])

            def w_high(uu):
                act.wait_ge(raw_ready[uu % 2], raw_count(uu))
                if uu >= 2:
                    v = uu - 2
                    if v < N_PROJ:
                        act.wait_ge(group_done, LAST_GROUP[v] + 1)
                    elif UNITS[v][1] == "gate":
                        act.wait_ge(gates_done, (v - N_PROJ) // 2 + 1)
                    elif UNITS[v][1] == "mix":
                        act.wait_ge(mix_done, (v - N_PROJ) // 2 + 1)
                    else:
                        act.wait_ge(y_done, 5 * (v - N_PROJ - 2 * (D // P) + 1))
                n = unit_cols(uu)
                act.activation(whi[:, uu % 2, 0:n], raw[:, uu % 2, 0:n], ACT.Copy).then_inc(w_hi, 1)

            for t, (t0, n) in enumerate(TILES):
                act.wait_ge(x_in[t], 16)
                if t >= 1:
                    act.wait_ge(x_sq, t)
                act.activation(wk[0:n, 2, 0:D], tm[0:n, t, :], ACT.Square, accum_out=xss[0:n, t:t + 1]).then_inc(x_sq, 1)
            w_high(0)
            for t, (t0, n) in enumerate(TILES):
                act.wait_ge(x_g, t + 1)
                act.activation(xhi[:, :, t0:t0 + n], wk[:, t % 2, 0:KC * n].rearrange("p (c n) -> p c n", c=KC),
                               ACT.Copy).then_inc(x_hi, 1)
            w_high(1)

            def evacuate(g):
                uu, part = GROUPS[g]
                name = UNITS[uu][0]
                act.wait_ge(group_done, g + 1)
                bank = ps[:, BANK[g], :]
                if name[:2] == "kw":
                    ins = act.activation(wk[0:KW, 3, HALF_NT * part[1]:HALF_NT * (part[1] + 1)], bank[0:KW, 0:HALF_NT], ACT.Copy)
                elif name[:2] == "qb":
                    f, h = part
                    p = 2 * int(name[2]) + f
                    c1 = min(HALF_NT * (h + 1), SEQ) - HALF_NT * h
                    for r, hh in ((0, 2 * p), (HD, 2 * p + 1)):
                        ins = act.activation(qT[r:r + HD, hh, HALF_NT * h:HALF_NT * h + c1], bank[r:r + HD, 0:c1],
                                             ACT.Copy, scale=HD ** -0.5)
                        if c1 < HALF_NT:
                            ins = act.activation(qS[r:r + HD, hh, :], bank[r:r + HD, c1:HALF_NT], ACT.Copy, scale=HD ** -0.5)
                elif name[0] == "u":
                    f, h = part
                    c = (4 if name[1] == "b" else 0) + 2 * int(name[2]) + f
                    if g == FIRST_GROUP[U["ua0"]]:
                        act.wait_ge(st_ka, 32)
                    ins = act.activation(u[:, c, HALF_NT * h:HALF_NT * (h + 1)], bank[:, 0:HALF_NT], ACT.Copy)
                else:
                    t, (t0, n) = part, TILES[part]
                    c = UC * int(name[2])
                    if name[0] == "v":
                        dst = vals[0:n, t if t < 4 else 6, c:c + UC]
                    else:
                        c += W if name[:2] == "ka" else 0
                        dst = tm[0:n, t, c:c + UC]
                    if g == FIRST_GROUP[U["va0"]]:
                        act.wait_ge(st_vb, 32)
                    if g == FIRST_GROUP[U["qa0"]]:
                        act.wait_ge(st_kb, 32)
                    if g == FIRST_GROUP[U["ka0"]]:
                        act.wait_ge(st_ki, 32)
                    ins = act.activation(dst, bank[0:n, 0:UC], ACT.Copy)
                ins.then_inc(group_out, 1)
                if g == LAST_GROUP[uu]:
                    w_high(uu + 2)

            def evacuate_unit(name, first=0):
                for g in range(FIRST_GROUP[U[name]] + first, LAST_GROUP[U[name]] + 1):
                    evacuate(g)

            def item(n):
                if n % 2:
                    return
                item_out(act, n).then_inc(item_act, 1)

            def item_out(eng, n):
                kind, p = ITEMS[n]
                eng.wait_ge(item_done, n + 1)
                bank = ps[:, n % ITEM_BANKS, :]
                if kind in ("iq", "aq"):
                    eng.activation(qT[0:HD, 2 * p, 0:SEQ], bank[0:HD, :], ACT.Copy)
                    return eng.activation(qT[HD:P, 2 * p + 1, 0:SEQ], bank[HD:P, :], ACT.Copy)
                if kind in ("iqs", "aqs"):
                    v = bank[:, 0:PAIRS * DEC].rearrange("p (c n) -> p c n", c=PAIRS)
                    eng.activation(qS[0:HD, 0:H:2, :], v[0:HD], ACT.Copy)
                    return eng.activation(qS[HD:P, 1:H:2, :], v[HD:P], ACT.Copy)
                if kind in ("ik", "bk", "ak"):
                    return eng.activation(kT[:, p, 0:SEQ], bank, ACT.Copy)
                return eng.activation(kT[:, p, SEQ:KEYS], bank[:, 0:SKEYS], ACT.Copy)

            evacuate_unit("kw")
            evacuate(FIRST_GROUP[U["qi0"]])
            act.wait_ge(kw_tr, 1)
            v = ps[:, 5, 0:5 * KW].rearrange("p (t n) -> p t n", t=5)
            act.activation(tm[:, 0:4, W:W + KW], v[:, 0:4, :], ACT.Copy)
            act.activation(tm[0:DEC, 4, W:W + KW], v[0:DEC, 4, :], ACT.Copy).then_inc(kw_out, 1)
            evacuate_unit("qi0", 1)
            evacuate_unit("qi1")
            evacuate_unit("vb0")
            act.wait_ge(const_ready, 6)
            for n in I_ITEMS:
                item(n)
            evacuate_unit("vb1")
            for n, (h, b) in enumerate(DOTS):
                act.wait_ge(dot_done, n + 1)
                if n >= 4:
                    act.wait_ge(acc_done, n - 3)
                m = DEC if b == "s" else P
                act.activation(wk[0:m, n % 4, 0:n_keys(b)], ps[0:m, n % 6, 0:n_keys(b)], ACT.Relu,
                               scale=HD ** -0.5).then_inc(relu_done, 1)
            evacuate_unit("kb0")
            evacuate_unit("kb1")
            evacuate_unit("qb0")
            for n in B_ITEMS:
                item(n)
            evacuate_unit("qb1")

            def softplus(s):
                act.wait_ge(z_done, s + 1)
                if s >= 1:
                    act.wait_ge(l_done, s)
                base = 1536 * (s % 2)
                t = wk[:, 0, :]
                spans = [(P, 0, PACK)] if s < H else [(P, 0, 512), (DEC, 512, 256)]
                for n, c, w in spans:
                    last = act.activation(t[0:n, c:c + w], flat[0:n, base + c:base + c + w], ACT.Abs)
                link(last)
                for n, c, w in spans:
                    last = act.activation(t[0:n, c:c + w], t[0:n, c:c + w], ACT.Exp, scale=-1.0)
                link(last)
                for n, c, w in spans:
                    last = act.activation(t[0:n, c:c + w], t[0:n, c:c + w], ACT.Ln, bias=1.0)
                last.then_inc(t_done, 1)

            def weights(s):
                act.wait_ge(c_done, s + 1)
                if s >= 2:
                    act.wait_ge(pv_done, s - 1)
                base = 1536 * (s % 2)
                for n, c, w in ([(P, 0, PACK)] if s < H else [(P, 0, 512), (DEC, 512, 256)]):
                    last = act.activation(wk[0:n, 3 + s % 2, c:c + w], flat[0:n, base + c:base + c + w], ACT.Exp)
                last.then_inc(a_done, 1)

            g = FIRST_GROUP[U["ka0"]]
            for s in range(11):
                for part in range(2):
                    if g <= LAST_GROUP[U["qa1"]]:
                        evacuate(g)
                        g += 1
                    if part == 0 and s < 9:
                        softplus(s)
                if 1 <= s <= 9:
                    weights(s - 1)
            evacuate_unit("va0")
            evacuate_unit("va1")
            for n in A_ITEMS:
                item(n)

            def exps(s):
                act.wait_ge(mx_done, s + 1)
                if s >= 1:
                    act.wait_ge(p_done, s)
                pr = wk[:, s % 2, :]
                parts = [(i, QOFF[i], n_keys(i)) for i in range(4)] if s < H else [(q, 512 * q, SKEYS) for q in range(2)]
                for i, c, w in parts:
                    last = act.activation(pr[:, c:c + w], pr[:, c:c + w], ACT.Exp, bias=nmx[:, i:i + 1],
                                          accum_out=esum[:, i:i + 1])
                last.then_inc(e_done, 1)

            def turned(s):
                act.wait_ge(pt_done, s + 1)
                if s >= 2:
                    act.wait_ge(av_done, s - 1)
                dst = wk[:, 2 + s % 2, :]
                if s < H:
                    last = act.activation(dst[:, 0:PACK], flat[:, 1536:1536 + PACK], ACT.Copy)
                else:
                    for q in range(2):
                        act.activation(dst[:, 512 * q:512 * q + 256], ps[:, 3 + q, 0:256], ACT.Copy)
                        last = act.activation(dst[0:DEC, 512 * q + 256:512 * q + 384], ps[0:DEC, 3 + q, 256:384], ACT.Copy)
                last.then_inc(pt_out, 1)

            g = FIRST_GROUP[U["ua0"]]
            for s in range(11):
                if s < 9:
                    exps(s)
                if s < H:
                    evacuate(g)
                    g += 1
                if 1 <= s <= 9:
                    turned(s - 1)
                if s < H:
                    evacuate(g)
                    g += 1

            act.wait_ge(av_done, 9)
            for k in range(4):
                c = (4, 6, 0, 2)[k]
                act.activation(sgu[:, c:c + 2, :], u[:, c:c + 2, :], ACT.Sigmoid).then_inc(u_sig, 1)
            for k in range(4):
                c = (4, 6, 0, 2)[k]
                act.wait_ge(os_done, k + 1)
                act.activation(ohi[:, c:c + 2, :], oT[:, c:c + 2, :], ACT.Copy).then_inc(o_hi, 1)

            for d in range(D // P):
                act.wait_ge(gates_done, d + 1)
                if d == 0:
                    act.wait_ge(o_lo, 4)
                else:
                    act.wait_ge(mixed, d)
                for f in range(2):
                    last = act.activation(sg[:, f, :].rearrange("p (a n) -> p a n", a=2),
                                          ps[:, 2 * f:2 * f + 2, 0:HALF_NT], ACT.Sigmoid)
                last.then_inc(gates_sig, 1)
                w_high(N_PROJ + 2 * d + 2)
                act.wait_ge(mixed, d + 1)
                act.activation(mhi[:, d, :], sg[:, 2, :], ACT.Copy).then_inc(m_hi, 1)
                w_high(N_PROJ + 2 * d + 3)
            for o in range(2, D // UC):
                w_high(N_PROJ + 2 * (D // P) + o)

        @block.vector
        def _(dve):
            chain = [0]

            def link(ins):
                chain[0] += 1
                ins.then_inc(dve_chain, 1)
                dve.wait_ge(dve_chain, chain[0])

            def w_low(uu):
                dve.wait_ge(w_hi, uu + 1)
                n = unit_cols(uu)
                dve.tensor_tensor(wlo[:, uu % 2, 0:n], raw[:, uu % 2, 0:n], whi[:, uu % 2, 0:n].bitcast(F32),
                                  ALU.subtract).then_inc(w_lo, 1)

            for t, (t0, n) in enumerate(TILES):
                dve.wait_ge(x_rs, t + 1)
                dve.tensor_scalar(tm[0:n, t, :], tm[0:n, t, :], xrs[0:n, t:t + 1], None, ALU.mult).then_inc(x_scaled, 1)
            dve.wait_ge(const_in, 80)

            def x_gain(t):
                t0, n = TILES[t]
                dve.wait_ge(x_tr, t + 1)
                if t >= 2:
                    dve.wait_ge(x_lo, t - 1)
                src = flat[:, 1024 * (t % 2):1024 * (t % 2) + D].rearrange("p (c n) -> p c n", c=KC)[:, :, 0:n]
                dst = wk[:, t % 2, 0:KC * n].rearrange("p (c n) -> p c n", c=KC)
                dve.tensor_tensor(dst, src, gx.unsqueeze(2).to_broadcast([P, KC, n]), ALU.mult).then_inc(x_g, 1)

            def x_low(t):
                t0, n = TILES[t]
                dve.wait_ge(x_hi, t + 1)
                src = wk[:, t % 2, 0:KC * n].rearrange("p (c n) -> p c n", c=KC)
                dve.tensor_tensor(xlo[:, :, t0:t0 + n], src, xhi[:, :, t0:t0 + n].bitcast(F32), ALU.subtract).then_inc(x_lo, 1)

            x_gain(0)
            for t in range(1, 5):
                x_gain(t)
                x_low(t - 1)
            x_low(4)
            for uu in range(4):
                w_low(uu)

            def rotate(x, tt):
                n, T, nh = x.shape[0], x.shape[1], x.shape[2]
                a = rot[0:n, 0, 0:T * nh * ROT].rearrange("p (t h r) -> p t h r", t=T, h=nh)
                b = rot[0:n, 1, 0:T * nh * ROT].rearrange("p (t h r) -> p t h r", t=T, h=nh)

                def table(c0, c1):
                    return rope[0:n, tt, c0:c1].unsqueeze(2).to_broadcast([n, T, nh, c1 - c0])

                dve.tensor_tensor(a, x[:, :, :, 0:ROT], table(0, ROT), ALU.mult)
                dve.tensor_tensor(b[:, :, :, 0:HR], x[:, :, :, HR:ROT], table(ROT, ROT + HR), ALU.mult)
                link(dve.tensor_tensor(b[:, :, :, HR:ROT], x[:, :, :, 0:HR], table(ROT + HR, 2 * ROT), ALU.mult))
                link(dve.tensor_tensor(x[:, :, :, 0:ROT], a, b, ALU.add))

            def heads(n, t0, t1, c, nh):
                return tm[0:n, t0:t1, c:c + HD * nh].rearrange("p t (h d) -> p t h d", h=nh)

            dve.wait_ge(kw_out, 1)
            dve.tensor_scalar(wis[:, 0:4, :], tm[:, 0:4, W + HD:W + KW], float(H) ** -0.5, None, ALU.mult)
            link(dve.tensor_scalar(wis[0:DEC, 4:5, :], tm[0:DEC, 4:5, W + HD:W + KW], float(H) ** -0.5, None, ALU.mult))
            for t, (t0, n) in enumerate(TILES):
                ki = tm[0:n, t, W:W + HD]
                last = dve.tensor_tensor_reduce(square[0:n, HD * t:HD * t + HD], ki, ki, 1.0, 0.0, ALU.mult, ALU.add,
                                                nss[0:n, t, 0:1])
            last.then_inc(ki_ss, 1)
            dve.wait_ge(ki_rs, 1)
            for t, (t0, n) in enumerate(TILES):
                ki = tm[0:n, t, W:W + HD]
                last = dve.scalar_tensor_tensor(ki, ki, nrs[0:n, t, 0:1], gk[0:n, 2, :], ALU.mult, ALU.mult)
            link(last)
            dve.wait_ge(group_out, LAST_GROUP[U["qi1"]] + 1)
            rotate(heads(P, 0, 4, 0, H + 1), slice(0, 4))
            rotate(heads(DEC, 4, 5, 0, H + 1), slice(4, 5))
            for c in range(2):
                dve.tensor_copy(tm[:, 0:4, 5 * P + HD * c:5 * P + HD * c + HD], tm[:, 0:4, W:W + HD])
                last = dve.tensor_copy(tm[0:DEC, 4, 5 * P + HD * c:5 * P + HD * c + HD], tm[0:DEC, 4, W:W + HD])
            last.then_inc(i_rows, 1)

            def item(n):
                if n % 2 == 0:
                    return
                kind, p = ITEMS[n]
                dve.wait_ge(item_done, n + 1)
                bank = ps[:, n % ITEM_BANKS, :]
                if kind in ("iq", "aq"):
                    dve.tensor_copy(qT[0:HD, 2 * p, 0:SEQ], bank[0:HD, :])
                    last = dve.tensor_copy(qT[HD:P, 2 * p + 1, 0:SEQ], bank[HD:P, :])
                elif kind in ("iqs", "aqs"):
                    v = bank[:, 0:PAIRS * DEC].rearrange("p (c n) -> p c n", c=PAIRS)
                    dve.tensor_copy(qS[0:HD, 0:H:2, :], v[0:HD])
                    last = dve.tensor_copy(qS[HD:P, 1:H:2, :], v[HD:P])
                elif kind in ("ik", "bk", "ak"):
                    last = dve.tensor_copy(kT[:, p, 0:SEQ], bank)
                else:
                    last = dve.tensor_copy(kT[:, p, SEQ:KEYS], bank[:, 0:SKEYS])
                last.then_inc(item_dve, 1)

            w_low(4)
            dve.wait_ge(const_ready, 6)
            for n in I_ITEMS:
                item(n)
            w_low(5)
            w_low(6)

            def scores(b):
                return bias_s[0:DEC, :] if b == "s" else bias[:, QOFF[b]:QOFF[b] + n_keys(b)]

            for n, (h, b) in enumerate(DOTS):
                dve.wait_ge(relu_done, n + 1)
                m, t = (DEC, 4) if b == "s" else (P, b)
                r, w = wk[0:m, n % 4, 0:n_keys(b)], wis[0:m, t, h:h + 1]
                if h == 0:
                    dve.tensor_scalar(scores(b), r, w, None, ALU.mult).then_inc(acc_done, 1)
                else:
                    dve.wait_ge(acc_done, n - 3)
                    dve.scalar_tensor_tensor(scores(b), r, w, scores(b), ALU.mult, ALU.add).then_inc(acc_done, 1)
            dve.wait_ge(acc_done, len(DOTS))
            for b in (3, 2, 1):
                dve.memset(scores(b)[0:CHUNK, n_keys(b) - CHUNK:n_keys(b)], NEG)
            link(dve.memset(bias[:, QOFF[0]:QOFF[0] + P], 0.0))
            link(dve.memset(bias[0:CHUNK, QOFF[0] + CHUNK:QOFF[0] + P], NEG))

            steps = [0]
            last_step = {}

            def topk_round(r):
                live = [b for b in SCORED if r < ROUNDS[b]]
                for k, what in enumerate(("max", "take")):
                    for b in live:
                        if b in last_step:
                            dve.wait_ge(topk_step, last_step[b])
                        m = DEC if b == "s" else P
                        t8 = top[0:m, SCORED.index(b), :]
                        if k == 0:
                            ins = dve.max(t8, scores(b))
                        else:
                            ins = dve.match_replace(scores(b), t8, scores(b), TAKEN)
                        ins.then_inc(topk_step, 1)
                        steps[0] += 1
                        last_step[b] = steps[0]

            def topk_end():
                dve.wait_ge(topk_step, steps[0])
                for b in SCORED:
                    last = dve.tensor_scalar(scores(b), scores(b), 0.9 * TAKEN, NEG, ALU.is_gt, ALU.mult)
                last.then_inc(bias_done, 1)

            rounds = iter(range(ROUNDS[3]))
            for _ in range(2):
                topk_round(next(rounds))
            for uu in (7, 8, 9):
                w_low(uu)
                for _ in range(3):
                    topk_round(next(rounds))
            for n in B_ITEMS:
                item(n)
            w_low(10)

            def norm_sums(c, ss):
                for t, (t0, n) in enumerate(TILES):
                    v = tm[0:n, t, c:c + W]
                    link(dve.tensor_tensor(square[0:n, :], v, v, ALU.mult))
                    link(dve.tensor_reduce(nss[0:n, t, :], square[0:n, :].rearrange("p (h d) -> p h d", h=H), AX.X, ALU.add))
                dve.sem_inc(ss, 1)

            def norm_scale(c, rs, r):
                dve.wait_ge(rs, 1)
                for n, t0, t1 in ((P, 0, 4), (DEC, 4, 5)):
                    v = heads(n, t0, t1, c, H)
                    last = dve.tensor_tensor(v, v, nrs[0:n, t0:t1, :].unsqueeze(3).to_broadcast([n, t1 - t0, H, HD]), ALU.mult)
                last.then_inc(r, 1)

            def norm_rotate(c, g, rows):
                dve.wait_ge(g, 1)
                rotate(heads(P, 0, 4, c, H), slice(0, 4))
                rotate(heads(DEC, 4, 5, c, H), slice(4, 5))
                dve.sem_inc(rows, 1)

            def softplus_sum(s):
                dve.wait_ge(t_done, s + 1)
                if s >= 2:
                    dve.wait_ge(c_done, s - 1)
                base = 1536 * (s % 2)
                for n, c, w in ([(P, 0, PACK)] if s < H else [(P, 0, 512), (DEC, 512, 256)]):
                    last = dve.scalar_tensor_tensor(wk[0:n, 1 + s % 2, c:c + w], flat[0:n, base + c:base + c + w], 0.0,
                                                    wk[0:n, 0, c:c + w], ALU.max, ALU.add)
                last.then_inc(l_done, 1)

            def weighed(s, done, out, c):
                dve.wait_ge(done, s + 1)
                if s < H:
                    dve.tensor_copy(oT[:, c + s // 2, 0:SEQ], ps[:, 6, :]).then_inc(out, 1)
                else:
                    dve.tensor_copy(oT[:, c:c + PAIRS, SEQ:NT],
                                    ps[:, 6, 0:PAIRS * DEC].rearrange("p (c n) -> p c n", c=PAIRS)).then_inc(out, 1)

            g = FIRST_GROUP[U["ka0"]]
            for s in range(11):
                if s < 9:
                    softplus_sum(s)
                for _ in range(2):
                    if g <= LAST_GROUP[U["qa1"]]:
                        if g == LAST_GROUP[GROUPS[g][0]]:
                            w_low(GROUPS[g][0] + 2)
                        g += 1
                if s >= 2 and (s % 2 or s - 2 == H):
                    weighed(s - 2, pv_done, pv_out, 4)
                if s < 3:
                    for r in rounds:
                        topk_round(r)
                        if r % 2 == 0:
                            break
                if s == 3:
                    for r in rounds:
                        topk_round(r)
                    topk_end()
                if s == 5:
                    dve.wait_ge(group_out, LAST_GROUP[U["ka1"]] + 1)
                    norm_sums(W, nk_ss)
                if s == 6:
                    norm_scale(W, nk_rs, nk_r)
                if s == 8:
                    norm_rotate(W, nk_g, k_rows)
            dve.wait_ge(group_out, LAST_GROUP[U["qa1"]] + 1)
            norm_sums(0, nq_ss)
            norm_scale(0, nq_rs, nq_r)
            w_low(U["va0"] + 2)
            norm_rotate(0, nq_g, q_rows)
            w_low(U["va1"] + 2)
            for n in A_ITEMS:
                item(n)

            def masked(s):
                dve.wait_ge(lg_done, s + 1)
                if s >= 2:
                    dve.wait_ge(pt_done, s - 1)
                if s >= 1:
                    dve.wait_ge(e_done, s)
                if s == H:
                    dve.wait_ge(bias_rep, 64)
                pr = wk[:, s % 2, :]
                if s < H:
                    parts = [(i, QOFF[i], n_keys(i), bias[:, QOFF[i]:QOFF[i] + n_keys(i)]) for i in range(4)]
                else:
                    parts = [(q, 512 * q, SKEYS, bias_r) for q in range(2)]
                for i, c, w, mask in parts:
                    last = dve.tensor_tensor_reduce(pr[:, c:c + w], flat[:, c:c + w], mask, 1.0, -3e38,
                                                    ALU.add, ALU.max, mx[:, i:i + 1])
                link(last)
                k = len(parts)
                dve.tensor_scalar(nmx[:, 0:k], mx[:, 0:k], -1.0, None, ALU.mult).then_inc(mx_done, 1)

            def normed(s):
                dve.wait_ge(e_done, s + 1)
                pr = wk[:, s % 2, :]
                parts = [(i, QOFF[i], n_keys(i)) for i in range(4)] if s < H else [(q, 512 * q, SKEYS) for q in range(2)]
                link(dve.reciprocal(rsum[:, 0:len(parts)], esum[:, 0:len(parts)]))
                for i, c, w in parts:
                    last = dve.tensor_scalar(pr[:, c:c + w], pr[:, c:c + w], rsum[:, i:i + 1], None, ALU.mult)
                last.then_inc(p_done, 1)

            g = FIRST_GROUP[U["ua0"]]
            for s in range(11):
                if s < 9:
                    masked(s)
                    normed(s)
                if s < H:
                    for _ in range(2):
                        if g == LAST_GROUP[GROUPS[g][0]]:
                            w_low(GROUPS[g][0] + 2)
                        g += 1
                if s >= 2 and (s % 2 or s - 2 == H):
                    weighed(s - 2, av_done, av_out, 0)

            for k in range(4):
                c = (4, 6, 0, 2)[k]
                dve.wait_ge(ou_done, k + 1)
                dve.wait_ge(u_sig, k + 1)
                dve.tensor_tensor(oT[:, c:c + 2, :], oT[:, c:c + 2, :], sgu[:, c:c + 2, :], ALU.mult).then_inc(os_done, 1)
            for k in range(4):
                c = (4, 6, 0, 2)[k]
                dve.wait_ge(o_hi, k + 1)
                dve.tensor_tensor(olo[:, c:c + 2, :], oT[:, c:c + 2, :], ohi[:, c:c + 2, :].bitcast(F32),
                                  ALU.subtract).then_inc(o_lo, 1)

            for d in range(D // P):
                w_low(N_PROJ + 2 * d + 2)
                dve.wait_ge(mix_done, d + 1)
                dve.wait_ge(gates_sig, d + 1)
                for f in range(2):
                    v = sg[:, f, :].rearrange("p (a n) -> p a n", a=2)
                    last = dve.tensor_tensor(v, v, ps[:, 4 + 2 * f:6 + 2 * f, 0:HALF_NT], ALU.mult)
                last.then_inc(mix_used, 1)
                dve.wait_ge(mix_used, d + 1)
                if d >= 1:
                    dve.wait_ge(m_lo, d)
                dve.tensor_tensor(sg[:, 2, :], sg[:, 0, :], sg[:, 1, :], ALU.add).then_inc(mixed, 1)
                dve.wait_ge(m_hi, d + 1)
                dve.tensor_tensor(mlo[:, d, :], sg[:, 2, :], mhi[:, d, :].bitcast(F32), ALU.subtract).then_inc(m_lo, 1)
                w_low(N_PROJ + 2 * d + 3)

            dve.wait_ge(res_in, 32)
            for g in range(20):
                o, t = divmod(g, 5)
                n = TILES[t][1]
                dve.wait_ge(y_done, g + 1)
                v = res[0:n, t, UC * o:UC * o + UC]
                dve.tensor_tensor(v, v, ps[0:n, g % 8, 0:UC], ALU.add).then_inc(y_out, 1)
                if t == 4 and o + 2 < D // UC:
                    w_low(N_PROJ + 2 * (D // P) + o + 2)

        @block.gpsimd
        def _(pool):
            chain = [0]

            def link(ins):
                chain[0] += 1
                ins.then_inc(pool_chain, 1)
                pool.wait_ge(pool_chain, chain[0])

            pool.memset(ident, 0.0).then_inc(const_ready, 1)
            pool.memset(tri, -1.0).then_inc(const_ready, 1)
            pool.memset(ones, -1.0).then_inc(const_ready, 1)
            pool.memset(half, -0.5)
            pool.wait_ge(const_ready, 3)
            pool.affine_select(ident, ident, [[-1, P]], ALU.not_equal, 1.0, base=0, channel_multiplier=1).then_inc(const_ready, 1)

            def inverse_root(out, sums, n, width, cols):
                link(pool.tensor_scalar(sums, sums, 1.0 / n, EPS, ALU.mult, ALU.add))
                return pool.tensor_tensor(out, sums, half[0:sums.shape[0], 0:cols] if width is None else width, ALU.pow)

            for t, (t0, n) in enumerate(TILES):
                pool.wait_ge(x_sq, t + 1)
                inverse_root(xrs[0:n, t:t + 1], xss[0:n, t:t + 1], D, None, 1).then_inc(x_rs, 1)
            pool.affine_select(tri, tri, [[-1, P]], ALU.is_ge, 0.0, base=0, channel_multiplier=1).then_inc(const_ready, 1)
            pool.wait_ge(const_ready, 5)
            for q in (qT, qS):
                link(pool.memset(q[HD:P, 0:H:2, :], 0.0))
                link(pool.memset(q[0:HD, 1:H:2, :], 0.0))
            pool.wait_ge(const_in, 80)
            pool.tensor_scalar(gk[:, 0, :], gk[:, 0, :], HD ** -0.5, 0.0, ALU.mult, ALU.add).then_inc(const_ready, 1)

            pool.wait_ge(ki_ss, 1)
            link(inverse_root(nrs[:, 0:4, 0], nss[:, 0:4, 0], HD, None, 4))
            inverse_root(nrs[0:DEC, 4:5, 0], nss[0:DEC, 4:5, 0], HD, None, 1).then_inc(ki_rs, 1)

            def diagonals(tile, keep):
                for j in range(4):
                    v = tile[:, KOFF[j]:KOFF[j] + P]
                    keep_last = pool.affine_select(v, v, [[1, P]], ALU.is_gt, 0.0, base=0, channel_multiplier=-1)
                return keep_last

            def diagonals_s(tile):
                v = tile[0:DEC, 512:768].rearrange("p (h n) -> p h n", h=H)
                return pool.affine_select(v, v, [[0, H], [1, DEC]], ALU.is_gt, 0.0, base=0, channel_multiplier=-1)

            def norm_root(ss, rs):
                pool.wait_ge(ss, 1)
                link(inverse_root(nrs[:, 0:4, :].rearrange("p t h -> p (t h)"), nss[:, 0:4, :].rearrange("p t h -> p (t h)"),
                                  HD, None, 4 * H))
                inverse_root(nrs[0:DEC, 4, :], nss[0:DEC, 4, :], HD, None, H).then_inc(rs, 1)

            def norm_gain(c, a, r, g):
                pool.wait_ge(r, 1)
                for n, t0, t1 in ((P, 0, 4), (DEC, 4, 5)):
                    v = tm[0:n, t0:t1, c:c + W].rearrange("p t (h d) -> p t h d", h=H)
                    gain = gk[0:n, a, :].unsqueeze(1).unsqueeze(1).to_broadcast([n, t1 - t0, H, HD])
                    last = pool.tensor_tensor(v, v, gain, ALU.mult)
                last.then_inc(g, 1)

            for s in range(10):
                if s < 9:
                    pool.wait_ge(l_done, s + 1)
                    tile = wk[:, 1 + s % 2, :]
                    (diagonals(tile, None) if s < H else diagonals_s(tile)).then_inc(lm_done, 1)
                if s >= 1:
                    pool.wait_ge(a_done, s)
                    tile = wk[:, 3 + (s - 1) % 2, :]
                    (diagonals(tile, None) if s - 1 < H else diagonals_s(tile)).then_inc(am_done, 1)
                if s == 5:
                    norm_root(nk_ss, nk_rs)
                if s == 6:
                    norm_gain(W, 1, nk_r, nk_g)
            norm_root(nq_ss, nq_rs)
            norm_gain(0, 0, nq_r, nq_g)

            pool.wait_ge(group_out, len(GROUPS))
            pool.wait_ge(pv_out, 5)
            for k in range(4):
                c = (4, 6, 0, 2)[k]
                if k == 2:
                    pool.wait_ge(av_out, 5)
                pool.tensor_tensor(oT[:, c:c + 2, :], oT[:, c:c + 2, :], u[:, c:c + 2, :], ALU.mult).then_inc(ou_done, 1)


_INS = ["x_prompt", "x_sample", "cache_a_k", "cache_a_v", "cache_idx_k", "cache_b_k", "cache_b_v", "norm_g", "w_in",
        "q_norm_g", "k_norm_g", "idx_k_norm_g", "w_a_out", "w_b_out", "w_o", "rope_const"]
_OUTS = [(1, SEQ, D), (1, DEC, D),
         (1, 1, SEQ, H, HD), (1, 1, SEQ, H, HD), (1, 1, SEQ, HD), (1, 1, SEQ, H, HD), (1, 1, SEQ, H, HD),
         (1, 1, DEC, H, HD), (1, 1, DEC, H, HD), (1, 1, DEC, HD), (1, 1, DEC, H, HD), (1, 1, DEC, H, HD)]


def rope_tables():
    half = HR
    freq = np.float32(500000.0) ** (-np.arange(half, dtype=np.float32) / np.float32(half))
    pos = np.zeros((5, P), np.float32)
    pos[0:4] = np.arange(SEQ, dtype=np.float32).reshape(4, P)
    pos[4, 0:DEC] = PAST + np.arange(DEC, dtype=np.float32)
    ang = pos[:, :, None] * freq[None, None, :].astype(np.float32)
    cos, sin = np.cos(ang), np.sin(ang)
    table = np.concatenate([cos, cos, -sin, sin], axis=-1).astype(np.float32)
    return np.ascontiguousarray(table.transpose(1, 0, 2))


def kernel(**inputs):
    import concourse.bacc as _bacc
    from concourse.bass_utils import run_bass_kernel_spmd as _run

    nc = _bacc.Bacc("TRN2", target_bir_lowering=False, num_devices=1)
    arrays, args = {}, []
    for name in _INS:
        if name == "rope_const":
            a = rope_tables()
        else:
            a = np.ascontiguousarray(inputs[name])
            if name == "norm_g":
                a = np.ascontiguousarray(a.reshape(KC, P).T)
            if name in ("q_norm_g", "k_norm_g", "idx_k_norm_g"):
                a = np.ascontiguousarray(np.broadcast_to(a, (P, HD)))
        arrays[f"in_{name}"] = a
        args.append(nc.dram_tensor(f"in_{name}", a.shape, mybir.dt.from_np(a.dtype), kind="ExternalInput").ap())
    for i, shape in enumerate(_OUTS):
        args.append(nc.dram_tensor(f"out_{i}", shape, F32, kind="ExternalOutput").ap())
    build(nc, *args)
    r = _run(nc, [arrays], core_ids=[0])
    return tuple(r.results[0][f"out_{i}"] for i in range(len(_OUTS)))
```

```python
from contextlib import ExitStack

import numpy as np

import concourse.bass as bass
from concourse import mybir

F32 = mybir.dt.float32
F32R = mybir.dt.float32r
BF16 = mybir.dt.bfloat16
ALU = mybir.AluOpType
ACT = mybir.ActivationFunctionType
AX = mybir.AxisListType

P = 128
D = 1024
KC = D // P
SEQ, DEC, PAST = 512, 32, 256
NT = SEQ + DEC
HALF_NT = NT // 2
H, HD = 8, 64
PAIRS = H // 2
W = H * HD
EC = W // P
CHUNK = 64
TOPK_P = min(256, SEQ // 4)
TOPK_S = min(256, (PAST + DEC) // 4)
SKEYS = PAST + DEC
KEYS = SEQ + SKEYS
EPS = 1e-6
NEG = -1e30
TAKEN = -3e38
ROT = HD // 4
HR = ROT // 2
UC = 256
XSLOT = [0, 1, 3, 4, 0]
TILES = [(0, P), (P, P), (2 * P, P), (3 * P, P), (SEQ, DEC)]

QA, KA, VA, UA, QI = (W * i for i in range(5))
KI = QI + W
WI = KI + HD
QB = WI + H
KB, VB, UB = QB + W, QB + 2 * W, QB + 3 * W
GA = QB + 4 * W
GB = GA + D
KW = HD + H

QOFF = {3: 0, 2: 512, 0: 896, 1: 1024}
KOFF = {0: 0, 1: 512, 3: 896, 2: 1024}
PACK = 1280

UNITS = [("kw", "kw"), ("qi0", "tm"), ("qi1", "tm"), ("vb0", "tm"), ("vb1", "tm"), ("kb0", "tm"),
         ("kb1", "tm"), ("qb0", "fm"), ("qb1", "fm"), ("ka0", "tm"), ("ka1", "tm"), ("qa0", "tm"),
         ("qa1", "tm"), ("va0", "tm"), ("va1", "tm"), ("ua0", "fm"), ("ua1", "fm"), ("ub0", "fm"),
         ("ub1", "fm")]
COL = {"kw": KI, "qi": QI, "vb": VB, "kb": KB, "qb": QB, "ka": KA, "qa": QA, "va": VA, "ua": UA, "ub": UB}
U = {name: i for i, (name, _) in enumerate(UNITS)}
N_PROJ = len(UNITS)
for _d in range(D // P):
    UNITS += [(f"gate{_d}", "gate"), (f"mix{_d}", "mix")]
UNITS += [(f"out{_o}", "out") for _o in range(D // UC)]

GROUPS = []
FIRST_GROUP, LAST_GROUP = {}, {}
for _u in range(N_PROJ):
    _kind = UNITS[_u][1]
    FIRST_GROUP[_u] = len(GROUPS)
    if _kind == "tm":
        GROUPS += [(_u, t) for t in range(5)]
    elif _kind == "kw":
        GROUPS += [(_u, (0, h)) for h in range(2)]
    else:
        GROUPS += [(_u, (f, h)) for f in range(UC // P) for h in range(2)]
    LAST_GROUP[_u] = len(GROUPS) - 1
BANK = []
for _g, (_u, _) in enumerate(GROUPS):
    _busy = U["ka0"] <= _u <= U["qa1"] or _u >= U["ua0"] or FIRST_GROUP[U["va0"]] <= _g < FIRST_GROUP[U["va0"]] + 2
    BANK.append(7 if _busy or _g % 2 else 6)


def unit_cols(u):
    kind = UNITS[u][1]
    return KC * KW if kind == "kw" else 2 * EC * P if kind == "mix" else KC * UC


def raw_count(u):
    return sum(32 if UNITS[v][1] in ("gate", "mix") else 16 for v in range(u % 2, u + 1, 2))


def sample_units(name):
    return sum(UNITS[v][1] == "tm" for v in range(U[name] + 1))


def group_evacuated_before(g):
    for p in range(g - 1, -1, -1):
        if BANK[p] == BANK[g]:
            return p + 1
    return 0


ITEMS = ([("iq", p) for p in range(PAIRS)] + [("iqs", 0), ("ik", 0), ("ikx", 0)]
         + [("bk", p) for p in range(PAIRS)] + [("bkx", p) for p in range(PAIRS)]
         + [("ak", p) for p in range(PAIRS)] + [("akx", p) for p in range(PAIRS)]
         + [("aq", p) for p in range(PAIRS)] + [("aqs", 0)])
I_ITEMS = range(0, 7)
B_ITEMS = range(7, 15)
A_ITEMS = range(15, 28)
ITEM_BANK = [3 + n - 23 if n >= 23 else n % 6 for n in range(len(ITEMS))]
ITEM_ON_ACT = [15 <= n < 23 or n % 2 == 0 for n in range(len(ITEMS))]


def by_act(n):
    return sum(ITEM_ON_ACT[:n])


def by_dve(n):
    return n - by_act(n)


SCORED = [3, 2, 1, "s"]
DOTS = [(h, b) for h in range(H) for b in SCORED]
ROUNDS = {3: TOPK_P // 8, 2: TOPK_P // 8, 1: TOPK_P // 8, "s": TOPK_S // 8}


def n_keys(b):
    return SKEYS if b == "s" else P * (b + 1)


def build(nc, x_prompt, x_sample, cache_a_k, cache_a_v, cache_idx_k, cache_b_k, cache_b_v, norm_g, w_in,
          q_norm_g, k_norm_g, idx_k_norm_g, w_a_out, w_b_out, w_o, rope_const,
          y_prompt, y_sample, new_a_k_p, new_a_v_p, new_idx_k_p, new_b_k_p, new_b_v_p,
          new_a_k_s, new_a_v_s, new_idx_k_s, new_b_k_s, new_b_v_s):
    with ExitStack() as ctx:
        place = [(nc.sbuf_base + 63) // 64 * 64]

        def sb_at(name, cols, dt, at):
            return nc.alloc_sbuf_tensor_at(name, [P, cols], dt, offset=at)

        def sb(name, cols, dt=F32):
            at = place[0]
            place[0] += (4 * cols + 31) // 32 * 32
            return sb_at(name, cols, dt, at)

        def sem(name):
            return ctx.enter_context(nc.semaphore(name))

        xhi = sb("xhi", KC * NT, F32R)[:, :].rearrange("p (c n) -> p c n", c=KC)
        xlo = sb("xlo", KC * NT, F32R)[:, :].rearrange("p (c n) -> p c n", c=KC)
        raw = sb("raw", 2 * KC * UC)[:, :].rearrange("p (s n) -> p s n", s=2)
        whi = sb("whi", 2 * KC * UC, F32R)[:, :].rearrange("p (s n) -> p s n", s=2)
        wlo = sb("wlo", 2 * KC * UC, F32R)[:, :].rearrange("p (s n) -> p s n", s=2)
        at_v = place[0]
        vals = sb("vals", 7 * W)[:, :].rearrange("p (t n) -> p t n", t=7)
        q_flat = sb("q_flat", H * NT)[:, :]
        qT = q_flat[:, 0:H * SEQ].rearrange("p (h n) -> p h n", h=H)
        qS = q_flat[:, H * SEQ:H * NT].rearrange("p (h n) -> p h n", h=H)
        kT = sb("kT", PAIRS * KEYS)[:, :].rearrange("p (c n) -> p c n", c=PAIRS)
        at_tm = place[0]
        tm = sb("tm", 5 * D)[:, :].rearrange("p (t n) -> p t n", t=5)
        at_wk = place[0]
        wk = sb("wk", 5 * PACK)[:, :].rearrange("p (s n) -> p s n", s=5)
        oT = sb("oT", 2 * PAIRS * NT)[:, :].rearrange("p (c n) -> p c n", c=2 * PAIRS)
        bias = sb("bias", PACK)[:, :]
        bias_s = sb("bias_s", SKEYS)[:, :]
        bias_r = sb("bias_r", SKEYS)[:, :]
        low_part = bias_r[:, 0:UC]
        square = sb("square", W)[:, :]
        rot = sb("rot", 2 * 4 * 9 * ROT)[:, :].rearrange("p (a n) -> p a n", a=2)
        ident = sb("ident", P)[:, :]
        tri = sb("tri", P, F32R)[:, :]
        ones = sb("ones", P, F32R)[:, :]
        ident_b = sb("ident_b", P // 2)[:, :].bitcast(BF16)
        later = sb("later", P // 2)[:, :].bitcast(BF16)
        tri_f, ones_f = square[:, 0:P], square[:, P:2 * P]
        xst = sb("xst", KC * 2 * DEC, F32R)[:, :].rearrange("p (c n) -> p c n", c=KC)
        rope = sb("rope", 5 * 32)[:, :].rearrange("p (t n) -> p t n", t=5)
        gk = sb("gk", 3 * HD)[:, :].rearrange("p (a n) -> p a n", a=3)
        gx = sb("gx", KC)[:, :]
        xss = sb("xss", 8)[:, :]
        xrs = sb("xrs", 8)[:, :]
        halves = sb("halves", 5 * H)[:, :]
        nss = sb("nss", 5 * H)[:, :].rearrange("p (t h) -> p t h", t=5)
        nrs = sb("nrs", 5 * H)[:, :].rearrange("p (t h) -> p t h", t=5)
        wis = sb("wis", 5 * H)[:, :].rearrange("p (t h) -> p t h", t=5)
        top = sb("top", 4 * 8)[:, :].rearrange("p (b n) -> p b n", b=4)
        mx = sb("mx", 8)[:, :]
        nmx = sb("nmx", 8)[:, :]
        esum = sb("esum", 8)[:, :]
        rsum = sb("rsum", 8)[:, :]
        assert place[0] <= nc.sbuf_usable_end, (place[0], nc.sbuf_usable_end)
        ohi = sb_at("ohi", 2 * PAIRS * NT, F32R, at_v)[:, :].rearrange("p (c n) -> p c n", c=2 * PAIRS)
        olo = sb_at("olo", 2 * PAIRS * NT, F32R, at_v + 8 * PAIRS * NT)[:, :].rearrange("p (c n) -> p c n", c=2 * PAIRS)
        assert at_v + 16 * PAIRS * NT <= at_tm
        res = sb_at("res", 5 * D, F32, at_v)[:, :].rearrange("p (t n) -> p t n", t=5)
        u = tm.rearrange("p t n -> p (t n)")[:, 0:H * NT].rearrange("p (c n) -> p c n", c=H)
        mhi = sb_at("mhi", KC * NT, F32R, at_tm)[:, :].rearrange("p (c n) -> p c n", c=KC)
        mlo = sb_at("mlo", KC * NT, F32R, at_tm + 4 * KC * NT)[:, :].rearrange("p (c n) -> p c n", c=KC)
        Llo = sb_at("Llo", PACK, F32R, at_wk + 4 * PACK)[:, :]
        Lhi = sb_at("Lhi", PACK, F32R, at_wk + 8 * PACK)[:, :]
        sg = oT
        sgu = wk.rearrange("p s n -> p (s n)")[:, 0:H * NT].rearrange("p (c n) -> p c n", c=H)

        PS = ctx.enter_context(nc.psum_tensor("PS", [P, 8 * 512], F32))
        ps = PS[:, :].rearrange("p (b n) -> p b n", b=8)
        flat = PS[:, :]

        x_in = [sem(f"x_in{t}") for t in range(5)]
        const_in = sem("const_in")
        gx_in = sem("gx_in")
        x_lo_pool = sem("x_lo_pool")
        cache_i_in = sem("cache_i_in")
        cache_bk_in = sem("cache_bk_in")
        cache_bv_in = sem("cache_bv_in")
        cache_ak_in = sem("cache_ak_in")
        cache_av_in = sem("cache_av_in")
        res_in = sem("res_in")
        raw_ready = [sem("raw_ready0"), sem("raw_ready1")]
        w_hi = sem("w_hi")
        w_lo = sem("w_lo")
        const_ready = sem("const_ready")
        x_sq = sem("x_sq")
        x_rs = sem("x_rs")
        x_scaled = sem("x_scaled")
        x_tr = sem("x_tr")
        x_g = sem("x_g")
        x_hi = sem("x_hi")
        x_lo = sem("x_lo")
        x_st, m_st, y_low = sem("x_st"), sem("m_st"), sem("y_low")
        sample_rows = sem("sample_rows")
        group_done = sem("group_done")
        group_out = sem("group_out")
        kw_tr = sem("kw_tr")
        kw_out = sem("kw_out")
        ki_ss = sem("ki_ss")
        ki_rs = sem("ki_rs")
        i_rows = sem("i_rows")
        item_done = sem("item_done")
        item_act = sem("item_act")
        item_dve = sem("item_dve")
        dot_done = sem("dot_done")
        relu_done = sem("relu_done")
        acc_done = sem("acc_done")
        topk_step = sem("topk_step")
        bias_done = sem("bias_done")
        bias_rep = sem("bias_rep")
        nk_ss, nk_rs, k_rows = (sem(n) for n in ("nk_ss", "nk_rs", "k_rows"))
        nq_ss, nq_rs, q_rows = (sem(n) for n in ("nq_ss", "nq_rs", "q_rows"))
        z_done, t_done, l_done, lm_done, c_done, a_done, pv_done, pv_out, lh_done = (
            sem(n) for n in ("z_done", "t_done", "l_done", "lm_done", "c_done", "a_done", "pv_done", "pv_out", "lh_done"))
        lg_done, mx_done, e_done, p_done, pt_done, pt_out, av_done, av_out = (
            sem(n) for n in ("lg_done", "mx_done", "e_done", "p_done", "pt_done", "pt_out", "av_done", "av_out"))
        u_sig, ou_done, os_done, o_hi, o_lo = (sem(n) for n in ("u_sig", "ou_done", "os_done", "o_hi", "o_lo"))
        gates_done, gates_sig, mix_done, mix_used, mixed, m_hi, m_lo = (
            sem(n) for n in ("gates_done", "gates_sig", "mix_done", "mix_used", "mixed", "m_hi", "m_lo"))
        y_done, y_out = sem("y_done"), sem("y_out")
        st_ki, st_kb, st_vb, st_ka, st_va, st_y = (sem(n) for n in ("st_ki", "st_kb", "st_vb", "st_ka", "st_va", "st_y"))
        act_chain, dve_chain, pool_chain = sem("act_chain"), sem("dve_chain"), sem("pool_chain")

        def u_group(g):
            name, (f, h) = UNITS[GROUPS[g][0]][0], GROUPS[g][1]
            c = (4 if name[1] == "b" else 0) + 2 * int(name[2]) + f
            return u[:, c, HALF_NT * h:HALF_NT * (h + 1)], ps[:, BANK[g], 0:HALF_NT]

        def wview(buf, uu):
            return buf[:, uu % 2, 0:unit_cols(uu)].rearrange(
                "p (c n) -> p c n", c=2 * EC if UNITS[uu][1] == "mix" else KC)

        def rows_p(ap):
            ap = ap.rearrange("a b s h d -> (a b s) (h d)") if len(ap.shape) == 5 else ap.rearrange("a b s d -> (a b s) d")
            return ap.rearrange("(t p) n -> p t n", p=P)

        def rows_s(ap):
            return ap.rearrange("a b s h d -> (a b s) (h d)") if len(ap.shape) == 5 else ap.rearrange("a b s d -> (a b s) d")

        def cached(ap):
            return rows_p(ap)

        xp = x_prompt.rearrange("b (t p) d -> p (b t) d", p=P)
        xs = x_sample.rearrange("b s d -> (b s) d")
        wi_v = w_in.rearrange("l (c p) e -> p (l c) e", p=P)
        wa_v = w_a_out.rearrange("l (c p) e -> p (l c) e", p=P)
        wb_v = w_b_out.rearrange("l (c p) e -> p (l c) e", p=P)
        wo_v = w_o.rearrange("l (c p) e -> p (l c) e", p=P)
        cstage_i = wk[:, 4, 0:256].rearrange("p (t n) -> p t n", t=2)
        cstage_b = wk[:, 4, 256:1280].rearrange("p (t n) -> p t n", t=2)
        cstage_a = cstage_b

        block = ctx.enter_context(nc.Block())

        @block.sync
        def _(sp):
            def load_unit(uu):
                if uu >= 2:
                    sp.wait_ge(w_lo, uu - 1)
                name, kind = UNITS[uu]
                dst, ready = wview(raw, uu), raw_ready[uu % 2]
                if kind in ("tm", "fm"):
                    c = COL[name[:2]] + UC * int(name[2])
                    sp.dma_start(dst, wi_v[:, :, c:c + UC]).then_inc(ready, 16)
                elif kind == "kw":
                    sp.dma_start(dst, wi_v[:, :, KI:KI + KW]).then_inc(ready, 16)
                elif kind == "gate":
                    c = P * int(name[4:])
                    sp.dma_start(dst[:, :, 0:P], wi_v[:, :, GA + c:GA + c + P]).then_inc(ready, 16)
                    sp.dma_start(dst[:, :, P:UC], wi_v[:, :, GB + c:GB + c + P]).then_inc(ready, 16)
                elif kind == "mix":
                    c = P * int(name[3:])
                    sp.dma_start(dst[:, 0:EC, :], wa_v[:, :, c:c + P]).then_inc(ready, 16)
                    sp.dma_start(dst[:, EC:2 * EC, :], wb_v[:, :, c:c + P]).then_inc(ready, 16)
                else:
                    c = UC * int(name[3:])
                    sp.dma_start(dst, wo_v[:, :, c:c + UC]).then_inc(ready, 16)

            for t in range(4):
                sp.dma_start(tm[:, t, :], xp[:, t, :]).then_inc(x_in[t], 16)
                if t == 0:
                    sp.dma_start(gx, norm_g).then_inc(gx_in, 16)
            sp.dma_start(tm[0:DEC, 4, :], xs).then_inc(x_in[4], 16)
            load_unit(0)
            sp.dma_start(rope, rope_const).then_inc(const_in, 16)
            sp.dma_start(gk[:, 0, :], q_norm_g).then_inc(const_in, 16)
            sp.dma_start(gk[:, 1, :], k_norm_g).then_inc(const_in, 16)
            sp.dma_start(gk[:, 2, :], idx_k_norm_g).then_inc(const_in, 16)

            for uu in range(1, 3):
                load_unit(uu)
            sp.wait_ge(x_lo_pool, 2)
            sp.wait_ge(x_lo, 3)
            for c in range(2):
                sp.dma_start(cstage_i[:, :, HD * c:HD * c + HD], cached(cache_idx_k)).then_inc(cache_i_in, 16)
            sp.dma_start(cstage_b, cached(cache_b_k)).then_inc(cache_bk_in, 16)
            sp.dma_start(vals[:, 4:6, :], cached(cache_b_v)).then_inc(cache_bv_in, 16)
            for uu in range(3, U["kb0"] + 1):
                load_unit(uu)
            sp.wait_ge(i_rows, 1)
            sp.dma_start(rows_p(new_idx_k_p), tm[:, 0:4, W:W + HD]).then_inc(st_ki, 16)
            sp.dma_start(rows_s(new_idx_k_s), tm[0:DEC, 4, W:W + HD]).then_inc(st_ki, 16)
            load_unit(U["kb1"])
            sp.wait_ge(group_out, LAST_GROUP[U["vb1"]] + 1)
            sp.wait_ge(sample_rows, sample_units("vb1"))
            sp.dma_start(rows_p(new_b_v_p), vals[:, 0:4, :]).then_inc(st_vb, 16)
            sp.dma_start(rows_s(new_b_v_s), vals[0:DEC, 6, :]).then_inc(st_vb, 16)
            load_unit(U["qb0"])
            load_unit(U["qb1"])
            sp.wait_ge(group_out, LAST_GROUP[U["kb1"]] + 1)
            sp.wait_ge(sample_rows, sample_units("kb1"))
            sp.dma_start(rows_p(new_b_k_p), tm[:, 0:4, 0:W]).then_inc(st_kb, 16)
            sp.dma_start(rows_s(new_b_k_s), tm[0:DEC, 4, 0:W]).then_inc(st_kb, 16)
            for uu in range(U["ka0"], U["va1"] + 1):
                load_unit(uu)
            sp.wait_ge(pv_done, 9)
            sp.dma_start(cstage_a, cached(cache_a_k)).then_inc(cache_ak_in, 16)
            sp.dma_start(vals[:, 4:6, :], cached(cache_a_v)).then_inc(cache_av_in, 16)
            load_unit(U["ua0"])
            sp.wait_ge(k_rows, 1)
            sp.dma_start(rows_p(new_a_k_p), tm[:, 0:4, W:2 * W]).then_inc(st_ka, 16)
            sp.dma_start(rows_s(new_a_k_s), tm[0:DEC, 4, W:2 * W]).then_inc(st_ka, 16)
            load_unit(U["ua1"])
            sp.wait_ge(group_out, LAST_GROUP[U["va1"]] + 1)
            sp.wait_ge(sample_rows, sample_units("va1"))
            sp.dma_start(rows_p(new_a_v_p), vals[:, 0:4, :]).then_inc(st_va, 16)
            sp.dma_start(rows_s(new_a_v_s), vals[0:DEC, 6, :]).then_inc(st_va, 16)
            sp.wait_ge(bias_done, 1)
            for r in range(4):
                sp.dma_start(bias_r[32 * r:32 * r + 32, :], bias_s[0:DEC, :]).then_inc(bias_rep, 16)
            for uu in range(U["ub0"], len(UNITS)):
                load_unit(uu)
                if UNITS[uu][0] == "out1":
                    sp.wait_ge(mix_done, D // P)
                    sp.dma_start(res[:, 0:4, :], xp).then_inc(res_in, 16)
                    sp.dma_start(res[0:DEC, 4, :], xs).then_inc(res_in, 16)
            yp = y_prompt.rearrange("b (t p) d -> p (b t) d", p=P)
            ys = y_sample.rearrange("b s d -> (b s) d")
            for g in range(20):
                o, t = divmod(g, 5)
                sp.wait_ge(y_out, g + 1)
                dst, n = (yp[:, t, :], P) if t < 4 else (ys, DEC)
                sp.dma_start(dst[:, UC * o:UC * o + UC], res[0:n, t, UC * o:UC * o + UC]).then_inc(st_y, 16)
            sp.wait_ge(st_y, 16 * 20)
            for s in (st_ki, st_kb, st_vb, st_ka, st_va):
                sp.wait_ge(s, 32)

        @block.tensor
        def _(pe):
            PASSES = ((0, 0), (0, 1), (1, 0))
            xpart, wpart = (xhi, xlo), (whi, wlo)

            pe.wait_ge(const_ready, 4)
            for t, (t0, n) in enumerate(TILES):
                pe.wait_ge(x_scaled, t + 1)
                if t >= 2:
                    pe.wait_ge(x_g, t - 1)
                for c in range(KC):
                    col = 1024 * (t % 2) + P * c
                    last = pe.transpose(flat[:, col:col + n], tm[0:n, t, P * c:P * c + P], ident[0:n, 0:n])
                last.then_inc(x_tr, 1)
            pe.wait_ge(x_lo, 1)
            pe.wait_ge(x_lo_pool, 2)

            def group(g):
                uu, part = GROUPS[g]
                if g == FIRST_GROUP[uu]:
                    pe.wait_ge(w_lo, uu + 1)
                if g == 1:
                    pe.wait_ge(x_lo, 3)
                if group_evacuated_before(g):
                    pe.wait_ge(group_out, group_evacuated_before(g))
                bank = ps[:, BANK[g], :]
                if UNITS[uu][1] == "tm" and part == 4:
                    pe.wait_ge(x_st, 1)
                    for c in range(KC):
                        for b in range(2):
                            mm = pe.matmul(bank[0:2 * DEC, 0:UC], xst[:, c, :], wview(wpart[b], uu)[:, c, :],
                                           start=(c + b == 0), stop=(c + b == KC))
                    mm.then_inc(group_done, 1)
                    return
                k = 0
                for c in range(KC):
                    for a, b in PASSES:
                        w = wview(wpart[b], uu)[:, c, :]
                        if UNITS[uu][1] == "tm":
                            t0, n = TILES[part]
                            out, lhsT, rhs = bank[0:n, 0:UC], xpart[a][:, c, t0:t0 + n], w
                        else:
                            f, h = part
                            m = KW if UNITS[uu][1] == "kw" else P
                            out, lhsT = bank[0:m, 0:HALF_NT], w[:, P * f:P * f + m]
                            rhs = xpart[a][:, c, HALF_NT * h:HALF_NT * (h + 1)]
                        mm = pe.matmul(out, lhsT, rhs, start=(k == 0), stop=(k == 23))
                        k += 1
                mm.then_inc(group_done, 1)

            def unit(name):
                for g in range(FIRST_GROUP[U[name]], LAST_GROUP[U[name]] + 1):
                    group(g)

            unit("kw")
            group(FIRST_GROUP[U["qi0"]])
            pe.wait_ge(group_out, LAST_GROUP[U["kw"]] + 1)
            for t, (t0, n) in enumerate(TILES):
                last = pe.transpose(ps[0:n, 5, KW * t:KW * t + KW], wk[0:KW, 3, t0:t0 + n], ident[0:KW, 0:KW])
            last.then_inc(kw_tr, 1)
            for g in range(FIRST_GROUP[U["qi0"]] + 1, LAST_GROUP[U["qi0"]] + 1):
                group(g)
            unit("qi1")
            unit("vb0")

            def item(n):
                kind, p = ITEMS[n]
                before = [m for m in range(n) if ITEM_BANK[m] == ITEM_BANK[n]]
                if before:
                    m = before[-1]
                    if ITEM_ON_ACT[m]:
                        pe.wait_ge(item_act, by_act(m + 1))
                    else:
                        pe.wait_ge(item_dve, by_dve(m + 1))
                bank = ps[:, ITEM_BANK[n], :]
                src = {"ik": 5 * P, "bk": P * p, "ak": W + P * p, "iq": P * p, "aq": P * p}
                if kind in src:
                    for t in range(4):
                        last = pe.transpose(bank[:, P * t:P * t + P], tm[:, t, src[kind]:src[kind] + P], ident)
                elif kind in ("iqs", "aqs"):
                    for q in range(PAIRS):
                        last = pe.transpose(bank[:, DEC * q:DEC * q + DEC], tm[0:DEC, 4, P * q:P * q + P],
                                            ident[0:DEC, 0:DEC])
                else:
                    s = src[kind[:2]]
                    stage = {"ikx": cstage_i, "bkx": cstage_b, "akx": cstage_a}[kind]
                    c = 0 if kind == "ikx" else P * p
                    for t in range(2):
                        pe.transpose(bank[:, P * t:P * t + P], stage[:, t, c:c + P], ident)
                    last = pe.transpose(bank[:, PAST:SKEYS], tm[0:DEC, 4, s:s + P], ident[0:DEC, 0:DEC])
                last.then_inc(item_done, 1)

            pe.wait_ge(i_rows, 1)
            pe.wait_ge(cache_i_in, 32)
            for n in I_ITEMS:
                item(n)
            unit("vb1")
            pe.wait_ge(item_act, by_act(I_ITEMS.stop))
            pe.wait_ge(item_dve, by_dve(I_ITEMS.stop))
            for n, (h, b) in enumerate(DOTS):
                if n >= 6:
                    pe.wait_ge(relu_done, n - 5)
                m, q, k0 = (DEC, qS[:, h, :], SEQ) if b == "s" else (P, qT[:, h, P * b:P * b + P], 0)
                pe.matmul(ps[0:m, n % 6, 0:n_keys(b)], q, kT[:, 0, k0:k0 + n_keys(b)],
                          start=True, stop=True).then_inc(dot_done, 1)
            unit("kb0")
            unit("kb1")
            unit("qb0")
            pe.wait_ge(relu_done, len(DOTS))
            pe.wait_ge(cache_bk_in, 16)
            pe.wait_ge(sample_rows, sample_units("kb1"))
            for n in B_ITEMS:
                item(n)
            unit("qb1")
            pe.wait_ge(group_out, LAST_GROUP[U["qb1"]] + 1)
            pe.wait_ge(item_act, by_act(B_ITEMS.stop))
            pe.wait_ge(item_dve, by_dve(B_ITEMS.stop))
            pe.wait_ge(cache_bv_in, 16)

            def z(s):
                if s >= 2:
                    pe.wait_ge(a_done, s - 1)
                base = 1536 * (s % 2)
                if s < H:
                    for j in (0, 1, 3, 2):
                        nq = SEQ - P * j
                        o = base + KOFF[j]
                        pe.matmul(flat[:, o:o + nq], kT[:, s // 2, P * j:P * j + P], qT[:, s, P * j:SEQ],
                                  start=(j != 3), stop=True, skip_group_check=True)
                    for j in range(4):
                        o = base + KOFF[j]
                        last = pe.matmul(flat[:, o:o + P], ident_b, later, start=False, stop=True, skip_group_check=True)
                else:
                    for b in range(3):
                        kn = P if b < 2 else DEC
                        for p in range(PAIRS):
                            o = base + 256 * b + 64 * p
                            last = pe.matmul(flat[0:kn, o:o + 64], kT[:, p, SEQ + P * b:SEQ + P * b + kn],
                                             q_flat[:, H * SEQ + 64 * p:H * SEQ + 64 * p + 64],
                                             start=(p == 0 and b != 1), stop=True,
                                             skip_group_check=True)
                    for h in range(H):
                        o = base + 512 + DEC * h
                        last = pe.matmul(flat[0:DEC, o:o + DEC], ident_b[0:DEC, 0:DEC], later[0:DEC, 0:DEC],
                                         start=False, stop=True, skip_group_check=True)
                last.then_inc(z_done, 1)

            def cumulate(s):
                pe.wait_ge(lm_done, s + 1)
                base = 1536 * (s % 2)
                for L in (Lhi, Llo):
                    if s < H:
                        for j in range(4):
                            nq = SEQ - P * j
                            last = pe.matmul(flat[:, base + KOFF[j]:base + KOFF[j] + nq], tri, L[:, KOFF[j]:KOFF[j] + nq],
                                             start=False, stop=True, skip_group_check=True)
                            for j2 in range(j + 1, 4):
                                n2 = SEQ - P * j2
                                o = base + KOFF[j] + P * (j2 - j)
                                last = pe.matmul(flat[:, o:o + n2], ones, L[:, KOFF[j2]:KOFF[j2] + n2],
                                                 start=False, stop=True, skip_group_check=True)
                    else:
                        for b in range(3):
                            kn = P if b < 2 else DEC
                            o = base + 256 * b
                            last = pe.matmul(flat[0:kn, o:o + 256], tri[0:kn, 0:kn], L[0:kn, 256 * b:256 * b + 256],
                                             start=False, stop=True, skip_group_check=True)
                            for b2 in range(b + 1, 3):
                                k2 = P if b2 < 2 else DEC
                                last = pe.matmul(flat[0:kn, o:o + 256], ones[0:k2, 0:kn],
                                                 L[0:k2, 256 * b2:256 * b2 + 256],
                                                 start=False, stop=True, skip_group_check=True)
                last.then_inc(c_done, 1)

            def weigh(s, probs, ready, out_ready, done, sample_col):
                pe.wait_ge(ready, s + 1)
                if s % 2 == 0 and s >= 2:
                    pe.wait_ge(out_ready, s // 2)
                if s < H:
                    r = HD * (s % 2)
                    for j in range(4):
                        last = pe.matmul(ps[r:r + HD, 6, P * j:SEQ], vals[:, j, HD * s:HD * s + HD],
                                         probs[:, KOFF[j]:KOFF[j] + SEQ - P * j], start=(j == 0), stop=(j == 3),
                                         skip_group_check=True)
                else:
                    for h in range(H):
                        r = HD * (h % 2)
                        for b in range(3):
                            kn = P if b < 2 else DEC
                            c = sample_col(h, b)
                            last = pe.matmul(ps[r:r + HD, 6, DEC * (h // 2):DEC * (h // 2) + DEC],
                                             vals[0:kn, 4 + b, HD * h:HD * h + HD], probs[0:kn, c:c + DEC],
                                             start=(b == 0), stop=(b == 2), skip_group_check=True)
                last.then_inc(done, 1)

            g = FIRST_GROUP[U["ka0"]]
            for s in range(11):
                for part in range(2):
                    group(g)
                    g += 1
                    if part == 0 and s < 9:
                        z(s)
                if 1 <= s <= 9:
                    cumulate(s - 1)
                if s >= 2:
                    weigh(s - 2, wk[:, 3 + s % 2, :], a_done, pv_out, pv_done, lambda h, b: 256 * b + DEC * h)
            pe.wait_ge(pv_out, 5)
            for g in range(g, LAST_GROUP[U["va0"]] + 1):
                group(g)
            unit("va1")

            pe.wait_ge(k_rows, 1)
            pe.wait_ge(cache_ak_in, 16)
            for n in A_ITEMS:
                if ITEMS[n] == ("aq", 0):
                    pe.wait_ge(q_rows, 1)
                    pe.wait_ge(group_out, LAST_GROUP[U["va1"]] + 1)
                item(n)
            pe.wait_ge(sample_rows, sample_units("va1"))
            pe.wait_ge(cache_av_in, 16)

            def logits(s):
                if s == 0:
                    pe.wait_ge(item_act, by_act(A_ITEMS.stop - PAIRS))
                    pe.wait_ge(item_dve, by_dve(A_ITEMS.stop - PAIRS))
                if s >= 1:
                    pe.wait_ge(mx_done, s)
                if s < H:
                    for i in (3, 2, 0, 1):
                        last = pe.matmul(flat[:, QOFF[i]:QOFF[i] + n_keys(i)], qT[:, s, P * i:P * i + P],
                                         kT[:, s // 2, 0:n_keys(i)], start=True, stop=True, skip_group_check=True)
                else:
                    for p in range(PAIRS):
                        r = HD * (p % 2)
                        last = pe.matmul(ps[r:r + HD, p // 2, 0:SKEYS], q_flat[:, H * SEQ + 64 * p:H * SEQ + 64 * p + 64],
                                         kT[:, p, SEQ:KEYS], start=True, stop=True)
                last.then_inc(lg_done, 1)

            def turn(s):
                pe.wait_ge(p_done, s + 1)
                if s >= 1:
                    pe.wait_ge(pt_out, s)
                pr = wk[:, s % 2, :]
                if s < H:
                    for i in range(4):
                        for j in range(i + 1):
                            o = 1536 + KOFF[j] + P * (i - j)
                            last = pe.transpose(flat[:, o:o + P], pr[:, QOFF[i] + P * j:QOFF[i] + P * j + P], ident)
                else:
                    for q in range(2):
                        for b in range(3):
                            kn = P if b < 2 else DEC
                            last = pe.transpose(ps[0:kn, 3 + q, P * b:P * b + P],
                                                pr[:, 512 * q + P * b:512 * q + P * b + kn], ident)
                last.then_inc(pt_done, 1)

            g = FIRST_GROUP[U["ua0"]]
            for s in range(11):
                if s < 9:
                    logits(s)
                if s == 0:
                    pe.wait_ge(item_act, by_act(A_ITEMS.stop))
                    pe.wait_ge(item_dve, by_dve(A_ITEMS.stop))
                if s < H:
                    group(g)
                    g += 1
                if 1 <= s <= 9:
                    turn(s - 1)
                if s < H:
                    group(g)
                    g += 1
                if s >= 2:
                    weigh(s - 2, wk[:, 2 + s % 2, :], pt_out, av_out, av_done,
                          lambda h, b: 512 * (h // 4) + P * b + DEC * (h % 4))

            pe.wait_ge(group_out, len(GROUPS))
            pe.wait_ge(av_out, 5)
            opart = (ohi, olo)
            for d in range(D // P):
                uu = N_PROJ + 2 * d
                pe.wait_ge(w_lo, uu + 1)
                if d >= 1:
                    pe.wait_ge(gates_sig, d)
                for f in range(2):
                    for h in range(2):
                        k = 0
                        for c in range(KC):
                            for a, b in PASSES:
                                mm = pe.matmul(ps[:, 2 * f + h, 0:HALF_NT], wview(wpart[b], uu)[:, c, P * f:P * f + P],
                                               xpart[a][:, c, HALF_NT * h:HALF_NT * (h + 1)], start=(k == 0), stop=(k == 23))
                                k += 1
                mm.then_inc(gates_done, 1)
                uu += 1
                if d == 0:
                    pe.wait_ge(o_lo, 4)
                pe.wait_ge(w_lo, uu + 1)
                if d >= 1:
                    pe.wait_ge(mix_used, d)
                for br in range(2):
                    for h in range(2):
                        k = 0
                        for c in range(EC):
                            for a, b in PASSES:
                                mm = pe.matmul(ps[:, 4 + 2 * br + h, 0:HALF_NT], wview(wpart[b], uu)[:, EC * br + c, :],
                                               opart[a][:, EC * br + c, HALF_NT * h:HALF_NT * (h + 1)],
                                               start=(k == 0), stop=(k == 11))
                                k += 1
                mm.then_inc(mix_done, 1)

            mpart = (mhi, mlo)

            def out_group(g, chunks):
                o, t = divmod(g, 5)
                uu = N_PROJ + 2 * (D // P) + o
                t0, n = TILES[t]
                for c in chunks:
                    if t < 4:
                        for a, b in PASSES:
                            mm = pe.matmul(ps[0:n, g % 8, 0:UC], mpart[a][:, c, t0:t0 + n], wview(wpart[b], uu)[:, c, :],
                                           start=(c + a + b == 0), stop=(c == KC - 1 and a == 1))
                    else:
                        for b in range(2):
                            mm = pe.matmul(ps[0:2 * DEC, g % 8, 0:UC], xst[:, c, :], wview(wpart[b], uu)[:, c, :],
                                           start=(c + b == 0), stop=(c + b == KC))
                return mm

            pe.wait_ge(gates_sig, D // P)
            pe.wait_ge(m_lo, D // P - 1)
            pe.wait_ge(w_lo, N_PROJ + 2 * (D // P) + 1)
            for g in range(3):
                out_group(g, range(KC - 1))
            pe.wait_ge(m_lo, D // P)
            for g in range(3):
                out_group(g, [KC - 1]).then_inc(y_done, 1)
            pe.wait_ge(mix_used, D // P)
            pe.wait_ge(m_st, 1)
            for g in range(3, 20):
                o, t = divmod(g, 5)
                if t == 0:
                    pe.wait_ge(w_lo, N_PROJ + 2 * (D // P) + o + 1)
                if g >= 8:
                    pe.wait_ge(y_out, g - 7)
                out_group(g, range(KC)).then_inc(y_done, 1)

        @block.scalar
        def _(act):
            chain = [0]

            def link(ins):
                chain[0] += 1
                ins.then_inc(act_chain, 1)
                act.wait_ge(act_chain, chain[0])

            def w_high(uu):
                act.wait_ge(raw_ready[uu % 2], raw_count(uu))
                if uu >= 2:
                    v = uu - 2
                    if v < N_PROJ:
                        act.wait_ge(group_done, LAST_GROUP[v] + 1)
                    elif UNITS[v][1] == "gate":
                        act.wait_ge(gates_done, (v - N_PROJ) // 2 + 1)
                    elif UNITS[v][1] == "mix":
                        act.wait_ge(mix_done, (v - N_PROJ) // 2 + 1)
                    else:
                        act.wait_ge(y_done, 5 * (v - N_PROJ - 2 * (D // P) + 1))
                n = unit_cols(uu)
                act.activation(whi[:, uu % 2, 0:n], raw[:, uu % 2, 0:n], ACT.Copy).then_inc(w_hi, 1)

            for t, (t0, n) in enumerate(TILES):
                act.wait_ge(x_in[t], 16)
                if t >= 1:
                    act.wait_ge(x_sq, t)
                act.activation(wk[0:n, 2, 0:D], tm[0:n, t, :], ACT.Square, accum_out=xss[0:n, t:t + 1]).then_inc(x_sq, 1)
            w_high(0)
            for t, (t0, n) in enumerate(TILES):
                act.wait_ge(x_g, t + 1)
                act.activation(xhi[:, :, t0:t0 + n], wk[:, XSLOT[t], 0:KC * n].rearrange("p (c n) -> p c n", c=KC),
                               ACT.Copy).then_inc(x_hi, 1)
            w_high(1)

            def evacuate(g, high=True):
                uu, part = GROUPS[g]
                name = UNITS[uu][0]
                act.wait_ge(group_done, g + 1)
                bank = ps[:, BANK[g], :]
                if name[:2] == "kw":
                    ins = act.activation(wk[0:KW, 3, HALF_NT * part[1]:HALF_NT * (part[1] + 1)], bank[0:KW, 0:HALF_NT], ACT.Copy)
                elif name[:2] == "qb":
                    f, h = part
                    p = 2 * int(name[2]) + f
                    c1 = min(HALF_NT * (h + 1), SEQ) - HALF_NT * h
                    for r, hh in ((0, 2 * p), (HD, 2 * p + 1)):
                        ins = act.activation(qT[r:r + HD, hh, HALF_NT * h:HALF_NT * h + c1], bank[r:r + HD, 0:c1],
                                             ACT.Copy, scale=HD ** -0.5)
                        if c1 < HALF_NT:
                            ins = act.activation(qS[r:r + HD, hh, :], bank[r:r + HD, c1:HALF_NT], ACT.Copy, scale=HD ** -0.5)
                else:
                    t, (t0, n) = part, TILES[part]
                    c = UC * int(name[2])
                    if name[0] == "v":
                        dst = vals[0:n, t if t < 4 else 6, c:c + UC]
                    else:
                        c += W if name[:2] == "ka" else 0
                        dst = tm[0:n, t, c:c + UC]
                    if g == FIRST_GROUP[U["va0"]]:
                        act.wait_ge(st_vb, 32)
                    if g == FIRST_GROUP[U["qa0"]]:
                        act.wait_ge(st_kb, 32)
                    if g == FIRST_GROUP[U["ka0"]]:
                        act.wait_ge(st_ki, 32)
                    ins = act.activation(dst, bank[0:n, 0:UC], ACT.Copy)
                    if t == 4:
                        k = sample_units(name)
                        if k >= 2:
                            act.wait_ge(sample_rows, k - 1)
                        ins = act.activation(low_part[0:DEC, :], bank[DEC:2 * DEC, 0:UC], ACT.Copy)
                ins.then_inc(group_out, 1)
                if g == LAST_GROUP[uu] and high:
                    w_high(uu + 2)

            def evacuate_unit(name, first=0, high=True):
                for g in range(FIRST_GROUP[U[name]] + first, LAST_GROUP[U[name]] + 1):
                    evacuate(g, high)

            def item(n):
                if not ITEM_ON_ACT[n]:
                    return
                item_out(act, n).then_inc(item_act, 1)

            def item_out(eng, n):
                kind, p = ITEMS[n]
                eng.wait_ge(item_done, n + 1)
                bank = ps[:, ITEM_BANK[n], :]
                if kind in ("iq", "aq"):
                    eng.activation(qT[0:HD, 2 * p, 0:SEQ], bank[0:HD, :], ACT.Copy)
                    return eng.activation(qT[HD:P, 2 * p + 1, 0:SEQ], bank[HD:P, :], ACT.Copy)
                if kind in ("iqs", "aqs"):
                    v = bank[:, 0:PAIRS * DEC].rearrange("p (c n) -> p c n", c=PAIRS)
                    eng.activation(qS[0:HD, 0:H:2, :], v[0:HD], ACT.Copy)
                    return eng.activation(qS[HD:P, 1:H:2, :], v[HD:P], ACT.Copy)
                if kind in ("ik", "bk", "ak"):
                    return eng.activation(kT[:, p, 0:SEQ], bank, ACT.Copy)
                return eng.activation(kT[:, p, SEQ:KEYS], bank[:, 0:SKEYS], ACT.Copy)

            evacuate_unit("kw")
            evacuate(FIRST_GROUP[U["qi0"]])
            act.wait_ge(kw_tr, 1)
            v = ps[:, 5, 0:5 * KW].rearrange("p (t n) -> p t n", t=5)
            act.activation(tm[:, 0:4, W:W + KW], v[:, 0:4, :], ACT.Copy)
            act.activation(tm[0:DEC, 4, W:W + KW], v[0:DEC, 4, :], ACT.Copy).then_inc(kw_out, 1)
            evacuate_unit("qi0", 1)
            evacuate_unit("qi1")
            evacuate_unit("vb0", high=False)
            act.wait_ge(const_ready, 6)
            for n in I_ITEMS:
                item(n)
            w_high(U["vb0"] + 2)
            evacuate_unit("vb1")
            for n, (h, b) in enumerate(DOTS):
                act.wait_ge(dot_done, n + 1)
                if n >= 4:
                    act.wait_ge(acc_done, n - 3)
                m = DEC if b == "s" else P
                act.activation(wk[0:m, n % 4, 0:n_keys(b)], ps[0:m, n % 6, 0:n_keys(b)], ACT.Relu,
                               scale=HD ** -0.5).then_inc(relu_done, 1)
            evacuate_unit("kb0")
            evacuate_unit("kb1")
            evacuate_unit("qb0", high=False)
            for n in B_ITEMS:
                item(n)
            w_high(U["qb0"] + 2)
            evacuate_unit("qb1", high=False)

            def softplus(s):
                act.wait_ge(z_done, s + 1)
                if s >= 1:
                    act.wait_ge(l_done, s)
                base = 1536 * (s % 2)
                t = wk[:, 0, :]
                spans = [(P, 0, PACK)] if s < H else [(P, 0, 512), (DEC, 512, 256)]
                for n, c, w in spans:
                    last = act.activation(t[0:n, c:c + w], flat[0:n, base + c:base + c + w], ACT.Abs)
                link(last)
                for n, c, w in spans:
                    last = act.activation(t[0:n, c:c + w], t[0:n, c:c + w], ACT.Exp, scale=-1.0)
                link(last)
                for n, c, w in spans:
                    last = act.activation(t[0:n, c:c + w], t[0:n, c:c + w], ACT.Ln, bias=1.0)
                last.then_inc(t_done, 1)

            def weights(s):
                act.wait_ge(c_done, s + 1)
                if s >= 2:
                    act.wait_ge(pv_done, s - 1)
                base = 1536 * (s % 2)
                for n, c, w in ([(P, 0, PACK)] if s < H else [(P, 0, 512), (DEC, 512, 256)]):
                    last = act.activation(wk[0:n, 3 + s % 2, c:c + w], flat[0:n, base + c:base + c + w], ACT.Exp)
                last.then_inc(a_done, 1)

            g = FIRST_GROUP[U["ka0"]]
            for s in range(11):
                for part in range(2):
                    if not (s < 2 and part):
                        evacuate(g, high=g != LAST_GROUP[U["qa1"]])
                    g += 1
                    if part == 0 and s < 9:
                        softplus(s)
                    if s == 0 and part == 0:
                        w_high(U["qb1"] + 2)
                if 1 <= s <= 9:
                    weights(s - 1)
                if s == 9:
                    w_high(U["qa1"] + 2)
            evacuate_unit("va0", 2)
            evacuate_unit("va1", high=False)
            for n in A_ITEMS:
                item(n)

            def exps(s):
                act.wait_ge(mx_done, s + 1)
                if s >= 1:
                    act.wait_ge(p_done, s)
                pr = wk[:, s % 2, :]
                parts = [(i, QOFF[i], n_keys(i)) for i in range(4)] if s < H else [(q, 512 * q, SKEYS) for q in range(2)]
                for i, c, w in parts:
                    last = act.activation(pr[:, c:c + w], pr[:, c:c + w], ACT.Exp, bias=nmx[:, i:i + 1],
                                          accum_out=esum[:, i:i + 1])
                last.then_inc(e_done, 1)

            def turned(s):
                act.wait_ge(pt_done, s + 1)
                if s >= 2:
                    act.wait_ge(av_done, s - 1)
                dst = wk[:, 2 + s % 2, :]
                if s < H:
                    last = act.activation(dst[:, 0:PACK], flat[:, 1536:1536 + PACK], ACT.Copy)
                else:
                    for q in range(2):
                        act.activation(dst[:, 512 * q:512 * q + 256], ps[:, 3 + q, 0:256], ACT.Copy)
                        last = act.activation(dst[0:DEC, 512 * q + 256:512 * q + 384], ps[0:DEC, 3 + q, 256:384], ACT.Copy)
                last.then_inc(pt_out, 1)

            g = FIRST_GROUP[U["ua0"]]
            for s in range(11):
                if s < 9:
                    exps(s)
                if s == 0:
                    w_high(U["va1"] + 2)
                if 1 <= s <= 9:
                    turned(s - 1)
                if s < H:
                    if s == 0:
                        act.wait_ge(st_ka, 32)
                    u_tile, bank = u_group(g + 1)
                    act.wait_ge(group_done, g + 2)
                    act.activation(u_tile, bank, ACT.Copy).then_inc(group_out, 1)
                    if g + 1 == LAST_GROUP[GROUPS[g + 1][0]]:
                        w_high(GROUPS[g + 1][0] + 2)
                    g += 2

            act.wait_ge(av_done, 9)
            for k in range(4):
                c = (4, 6, 0, 2)[k]
                act.activation(sgu[:, c:c + 2, :], u[:, c:c + 2, :], ACT.Sigmoid).then_inc(u_sig, 1)
            for k in range(4):
                c = (4, 6, 0, 2)[k]
                act.wait_ge(os_done, k + 1)
                act.activation(ohi[:, c:c + 2, :], oT[:, c:c + 2, :], ACT.Copy).then_inc(o_hi, 1)

            for d in range(D // P):
                act.wait_ge(gates_done, d + 1)
                if d == 0:
                    act.wait_ge(o_lo, 4)
                else:
                    act.wait_ge(mixed, d)
                for f in range(2):
                    last = act.activation(sg[:, f, :].rearrange("p (a n) -> p a n", a=2),
                                          ps[:, 2 * f:2 * f + 2, 0:HALF_NT], ACT.Sigmoid)
                last.then_inc(gates_sig, 1)
                w_high(N_PROJ + 2 * d + 2)
                act.wait_ge(mixed, d + 1)
                act.activation(mhi[:, d, :], sg[:, 2, :], ACT.Copy).then_inc(m_hi, 1)
                w_high(N_PROJ + 2 * d + 3)
            for o in range(D // UC):
                if o >= 1 and o + 1 < D // UC:
                    w_high(N_PROJ + 2 * (D // P) + o + 1)
                g = 5 * o + 4
                act.wait_ge(y_done, g + 1)
                if o >= 1:
                    act.wait_ge(y_out, g - 4)
                act.activation(low_part[0:DEC, :], ps[DEC:2 * DEC, g % 8, 0:UC], ACT.Copy).then_inc(y_low, 1)

        @block.vector
        def _(dve):
            chain = [0]

            def link(ins):
                chain[0] += 1
                ins.then_inc(dve_chain, 1)
                dve.wait_ge(dve_chain, chain[0])

            def w_low(uu):
                dve.wait_ge(w_hi, uu + 1)
                n = unit_cols(uu)
                dve.tensor_tensor(wlo[:, uu % 2, 0:n], raw[:, uu % 2, 0:n], whi[:, uu % 2, 0:n].bitcast(F32),
                                  ALU.subtract).then_inc(w_lo, 1)

            def x_scale(t):
                t0, n = TILES[t]
                dve.wait_ge(x_rs, t + 1)
                dve.tensor_scalar(tm[0:n, t, :], tm[0:n, t, :], xrs[0:n, t:t + 1], None, ALU.mult).then_inc(x_scaled, 1)

            def x_gain(t):
                t0, n = TILES[t]
                dve.wait_ge(x_tr, t + 1)
                if t == 4:
                    dve.wait_ge(x_lo_pool, 1)
                src = flat[:, 1024 * (t % 2):1024 * (t % 2) + D].rearrange("p (c n) -> p c n", c=KC)[:, :, 0:n]
                dst = wk[:, XSLOT[t], 0:KC * n].rearrange("p (c n) -> p c n", c=KC)
                dve.tensor_tensor(dst, src, gx.unsqueeze(2).to_broadcast([P, KC, n]), ALU.mult).then_inc(x_g, 1)

            def x_low(t):
                t0, n = TILES[t]
                dve.wait_ge(x_hi, t + 1)
                src = wk[:, XSLOT[t], 0:KC * n].rearrange("p (c n) -> p c n", c=KC)
                dve.tensor_tensor(xlo[:, :, t0:t0 + n], src, xhi[:, :, t0:t0 + n].bitcast(F32), ALU.subtract).then_inc(x_lo, 1)

            x_scale(0)
            x_scale(1)
            dve.wait_ge(gx_in, 16)
            x_gain(0)
            x_scale(2)
            x_gain(1)
            x_scale(3)
            x_gain(2)
            x_scale(4)
            w_low(0)
            x_low(1)
            x_gain(3)
            x_gain(4)
            x_low(3)
            x_low(4)
            dve.wait_ge(const_in, 64)
            for uu in range(1, 4):
                w_low(uu)

            def rotate(x, tt):
                n, T, nh = x.shape[0], x.shape[1], x.shape[2]
                a = rot[0:n, 0, 0:T * nh * ROT].rearrange("p (t h r) -> p t h r", t=T, h=nh)
                b = rot[0:n, 1, 0:T * nh * ROT].rearrange("p (t h r) -> p t h r", t=T, h=nh)

                def table(c0, c1):
                    return rope[0:n, tt, c0:c1].unsqueeze(2).to_broadcast([n, T, nh, c1 - c0])

                dve.tensor_tensor(a, x[:, :, :, 0:ROT], table(0, ROT), ALU.mult)
                dve.tensor_tensor(b[:, :, :, 0:HR], x[:, :, :, HR:ROT], table(ROT, ROT + HR), ALU.mult)
                link(dve.tensor_tensor(b[:, :, :, HR:ROT], x[:, :, :, 0:HR], table(ROT + HR, 2 * ROT), ALU.mult))
                link(dve.tensor_tensor(x[:, :, :, 0:ROT], a, b, ALU.add))

            def heads(n, t0, t1, c, nh):
                return tm[0:n, t0:t1, c:c + HD * nh].rearrange("p t (h d) -> p t h d", h=nh)

            dve.wait_ge(kw_out, 1)
            dve.wait_ge(const_ready, 6)
            dve.tensor_scalar(wis[:, 0:4, :], tm[:, 0:4, W + HD:W + KW], float(H) ** -0.5, None, ALU.mult)
            link(dve.tensor_scalar(wis[0:DEC, 4:5, :], tm[0:DEC, 4:5, W + HD:W + KW], float(H) ** -0.5, None, ALU.mult))
            for t, (t0, n) in enumerate(TILES):
                ki = tm[0:n, t, W:W + HD]
                last = dve.tensor_tensor_reduce(square[0:n, HD * t:HD * t + HD], ki, ki, 1.0, 0.0, ALU.mult, ALU.add,
                                                nss[0:n, t, 0:1])
            last.then_inc(ki_ss, 1)
            dve.wait_ge(ki_rs, 1)
            for t, (t0, n) in enumerate(TILES):
                ki = tm[0:n, t, W:W + HD]
                last = dve.scalar_tensor_tensor(ki, ki, nrs[0:n, t, 0:1], gk[0:n, 2, :], ALU.mult, ALU.mult)
            link(last)
            dve.wait_ge(group_out, LAST_GROUP[U["qi1"]] + 1)
            dve.wait_ge(sample_rows, sample_units("qi1"))
            rotate(heads(P, 0, 4, 0, H + 1), slice(0, 4))
            rotate(heads(DEC, 4, 5, 0, H + 1), slice(4, 5))
            for c in range(2):
                dve.tensor_copy(tm[:, 0:4, 5 * P + HD * c:5 * P + HD * c + HD], tm[:, 0:4, W:W + HD])
                last = dve.tensor_copy(tm[0:DEC, 4, 5 * P + HD * c:5 * P + HD * c + HD], tm[0:DEC, 4, W:W + HD])
            last.then_inc(i_rows, 1)

            def item(n):
                if ITEM_ON_ACT[n]:
                    return
                kind, p = ITEMS[n]
                dve.wait_ge(item_done, n + 1)
                bank = ps[:, ITEM_BANK[n], :]
                if kind in ("iq", "aq"):
                    dve.tensor_copy(qT[0:HD, 2 * p, 0:SEQ], bank[0:HD, :])
                    last = dve.tensor_copy(qT[HD:P, 2 * p + 1, 0:SEQ], bank[HD:P, :])
                elif kind in ("iqs", "aqs"):
                    v = bank[:, 0:PAIRS * DEC].rearrange("p (c n) -> p c n", c=PAIRS)
                    dve.tensor_copy(qS[0:HD, 0:H:2, :], v[0:HD])
                    last = dve.tensor_copy(qS[HD:P, 1:H:2, :], v[HD:P])
                elif kind in ("ik", "bk", "ak"):
                    last = dve.tensor_copy(kT[:, p, 0:SEQ], bank)
                else:
                    last = dve.tensor_copy(kT[:, p, SEQ:KEYS], bank[:, 0:SKEYS])
                last.then_inc(item_dve, 1)

            w_low(4)
            dve.wait_ge(const_ready, 6)
            for n in I_ITEMS:
                item(n)
            w_low(5)
            w_low(6)

            def scores(b):
                return bias_s[0:DEC, :] if b == "s" else bias[:, QOFF[b]:QOFF[b] + n_keys(b)]

            for n, (h, b) in enumerate(DOTS):
                dve.wait_ge(relu_done, n + 1)
                m, t = (DEC, 4) if b == "s" else (P, b)
                r, w = wk[0:m, n % 4, 0:n_keys(b)], wis[0:m, t, h:h + 1]
                if h == 0:
                    dve.tensor_scalar(scores(b), r, w, None, ALU.mult).then_inc(acc_done, 1)
                else:
                    dve.wait_ge(acc_done, n - 3)
                    dve.scalar_tensor_tensor(scores(b), r, w, scores(b), ALU.mult, ALU.add).then_inc(acc_done, 1)
            dve.wait_ge(acc_done, len(DOTS))
            for b in (3, 2, 1):
                dve.memset(scores(b)[0:CHUNK, n_keys(b) - CHUNK:n_keys(b)], NEG)
            link(dve.memset(bias[:, QOFF[0]:QOFF[0] + P], 0.0))
            link(dve.memset(bias[0:CHUNK, QOFF[0] + CHUNK:QOFF[0] + P], NEG))

            steps = [0]
            last_step = {}

            def topk_round(r):
                live = [b for b in SCORED if r < ROUNDS[b]]
                for k, what in enumerate(("max", "take")):
                    for b in live:
                        if b in last_step:
                            dve.wait_ge(topk_step, last_step[b])
                        m = DEC if b == "s" else P
                        t8 = top[0:m, SCORED.index(b), :]
                        if k == 0:
                            ins = dve.max(t8, scores(b))
                        else:
                            ins = dve.match_replace(scores(b), t8, scores(b), TAKEN)
                        ins.then_inc(topk_step, 1)
                        steps[0] += 1
                        last_step[b] = steps[0]

            def topk_end():
                dve.wait_ge(topk_step, steps[0])
                for b in SCORED:
                    last = dve.tensor_scalar(scores(b), scores(b), 0.9 * TAKEN, NEG, ALU.is_gt, ALU.mult)
                last.then_inc(bias_done, 1)

            rounds = iter(range(ROUNDS[3]))
            for uu in (7, 8):
                w_low(uu)
                for _ in range(10 - uu):
                    topk_round(next(rounds))
            for n in B_ITEMS:
                item(n)
            w_low(9)
            for _ in range(2):
                topk_round(next(rounds))

            def norm_sums(c, half, ss):
                h0, w = 4 * half, W // 2
                for t, (t0, n) in enumerate(TILES):
                    v = tm[0:n, t, c + w * half:c + w * half + w]
                    sq = square[0:n, w * (t % 2):w * (t % 2) + w]
                    link(dve.tensor_tensor(sq, v, v, ALU.mult))
                    last = dve.tensor_reduce(nss[0:n, t, h0:h0 + 4], sq.rearrange("p (h d) -> p h d", h=4), AX.X, ALU.add)
                    if t % 2:
                        link(last)
                link(last)
                dve.sem_inc(ss, 1)

            def half_heads(n, t0, t1, c, half):
                return heads(n, t0, t1, c + half * W // 2, 4)

            def norm_scale(c, half, rs):
                dve.wait_ge(rs, half + 1)
                for n, t0, t1 in ((P, 0, 4), (DEC, 4, 5)):
                    v = half_heads(n, t0, t1, c, half)
                    root = nrs[0:n, t0:t1, 4 * half:4 * half + 4].unsqueeze(3).to_broadcast([n, t1 - t0, 4, HD])
                    last = dve.tensor_tensor(v, v, root, ALU.mult)
                link(last)

            def norm_gain(c, half, a):
                for n, t0, t1 in ((P, 0, 4), (DEC, 4, 5)):
                    v = half_heads(n, t0, t1, c, half)
                    gain = gk[0:n, a, :].unsqueeze(1).unsqueeze(1).to_broadcast([n, t1 - t0, 4, HD])
                    last = dve.tensor_tensor(v, v, gain, ALU.mult)
                link(last)

            def norm_rotate(c, rows):
                rotate(heads(P, 0, 4, c, H), slice(0, 4))
                rotate(heads(DEC, 4, 5, c, H), slice(4, 5))
                dve.sem_inc(rows, 1)

            def spans(s):
                return [(P, 0, PACK)] if s < H else [(P, 0, 512), (DEC, 512, 256)]

            def softplus_sum(s):
                dve.wait_ge(t_done, s + 1)
                if s >= 1:
                    dve.wait_ge(c_done, s)
                base = 1536 * (s % 2)
                for n, c, w in ([(P, 0, PACK)] if s < H else [(P, 0, 512), (DEC, 512, 256)]):
                    last = dve.scalar_tensor_tensor(wk[0:n, 1, c:c + w], flat[0:n, base + c:base + c + w], 0.0,
                                                    wk[0:n, 0, c:c + w], ALU.max, ALU.add)
                last.then_inc(l_done, 1)
                dve.wait_ge(l_done, s + 1)
                for n, c, w in spans(s):
                    last = dve.tensor_copy(Lhi[0:n, c:c + w], wk[0:n, 1, c:c + w])
                last.then_inc(lh_done, 1)

            def weighed(s, done, out, c):
                dve.wait_ge(done, s + 1)
                if s < H:
                    dve.tensor_copy(oT[:, c + s // 2, 0:SEQ], ps[:, 6, :]).then_inc(out, 1)
                else:
                    dve.tensor_copy(oT[:, c:c + PAIRS, SEQ:NT],
                                    ps[:, 6, 0:PAIRS * DEC].rearrange("p (c n) -> p c n", c=PAIRS)).then_inc(out, 1)

            g = FIRST_GROUP[U["ka0"]]
            for s in range(11):
                if s < 2:
                    t = GROUPS[g + 1][1]
                    if s == 0:
                        dve.wait_ge(st_ki, 32)
                    dve.wait_ge(group_done, g + 2)
                    dve.tensor_copy(tm[:, t, W:W + UC], ps[:, BANK[g + 1], 0:UC]).then_inc(group_out, 1)
                if s < 9:
                    softplus_sum(s)
                if s == 0:
                    w_low(U["qb1"] + 2)
                for _ in range(2):
                    if g <= LAST_GROUP[U["qa1"]] and g == LAST_GROUP[GROUPS[g][0]]:
                        w_low(GROUPS[g][0] + 2)
                    g += 1
                if s >= 2 and (s % 2 or s - 2 == H):
                    weighed(s - 2, pv_done, pv_out, 4)
                if s < 5:
                    for _ in range(1 if s < 1 else 2):
                        topk_round(next(rounds))
                if s == 5:
                    topk_end()
                if s == 5:
                    dve.wait_ge(group_out, LAST_GROUP[U["ka1"]] + 1)
                    dve.wait_ge(sample_rows, sample_units("ka1"))
                    norm_sums(W, 0, nk_ss)
                    norm_sums(W, 1, nk_ss)
                if s == 7:
                    norm_scale(W, 0, nk_rs)
                    norm_scale(W, 1, nk_rs)
                if s == 8:
                    norm_gain(W, 0, 1)
                    norm_gain(W, 1, 1)
                if s == 9:
                    norm_rotate(W, k_rows)
            dve.wait_ge(group_out, LAST_GROUP[U["qa1"]] + 1)
            dve.wait_ge(sample_rows, sample_units("qa1"))
            norm_sums(0, 0, nq_ss)
            norm_sums(0, 1, nq_ss)
            for half in range(2):
                norm_scale(0, half, nq_rs)
                norm_gain(0, half, 0)
            norm_rotate(0, q_rows)
            w_low(U["va0"] + 2)
            for n in A_ITEMS:
                item(n)

            def masked(s):
                dve.wait_ge(lg_done, s + 1)
                if s >= 2:
                    dve.wait_ge(pt_done, s - 1)
                if s >= 1:
                    dve.wait_ge(e_done, s)
                if s == H:
                    dve.wait_ge(bias_rep, 64)
                pr = wk[:, s % 2, :]
                if s < H:
                    parts = [(i, QOFF[i], n_keys(i), bias[:, QOFF[i]:QOFF[i] + n_keys(i)]) for i in range(4)]
                else:
                    parts = [(q, 512 * q, SKEYS, bias_r) for q in range(2)]
                for i, c, w, mask in parts:
                    last = dve.tensor_tensor_reduce(pr[:, c:c + w], flat[:, c:c + w], mask, 1.0, -3e38,
                                                    ALU.add, ALU.max, mx[:, i:i + 1])
                link(last)
                k = len(parts)
                dve.tensor_scalar(nmx[:, 0:k], mx[:, 0:k], -1.0, None, ALU.mult).then_inc(mx_done, 1)

            def normed(s):
                dve.wait_ge(e_done, s + 1)
                pr = wk[:, s % 2, :]
                parts = [(i, QOFF[i], n_keys(i)) for i in range(4)] if s < H else [(q, 512 * q, SKEYS) for q in range(2)]
                link(dve.reciprocal(rsum[:, 0:len(parts)], esum[:, 0:len(parts)]))
                for i, c, w in parts:
                    last = dve.tensor_scalar(pr[:, c:c + w], pr[:, c:c + w], rsum[:, i:i + 1], None, ALU.mult)
                last.then_inc(p_done, 1)

            g = FIRST_GROUP[U["ua0"]]
            for s in range(11):
                if s < 9:
                    masked(s)
                if s < H:
                    if s == 0:
                        dve.wait_ge(st_ka, 32)
                    u_tile, bank = u_group(g)
                    dve.wait_ge(group_done, g + 1)
                    dve.tensor_copy(u_tile, bank).then_inc(group_out, 1)
                if s < 9:
                    normed(s)
                if s == 0:
                    w_low(U["va1"] + 2)
                if s < H:
                    if g + 1 == LAST_GROUP[GROUPS[g + 1][0]]:
                        w_low(GROUPS[g + 1][0] + 2)
                    g += 2
                if s >= 2 and (s % 2 or s - 2 == H):
                    weighed(s - 2, av_done, av_out, 0)

            for k in range(4):
                c = (4, 6, 0, 2)[k]
                dve.wait_ge(ou_done, k + 1)
                dve.wait_ge(u_sig, k + 1)
                dve.tensor_tensor(oT[:, c:c + 2, :], oT[:, c:c + 2, :], sgu[:, c:c + 2, :], ALU.mult).then_inc(os_done, 1)
            for k in range(4):
                c = (4, 6, 0, 2)[k]
                dve.wait_ge(o_hi, k + 1)
                dve.tensor_tensor(olo[:, c:c + 2, :], oT[:, c:c + 2, :], ohi[:, c:c + 2, :].bitcast(F32),
                                  ALU.subtract).then_inc(o_lo, 1)

            for d in range(D // P):
                w_low(N_PROJ + 2 * d + 2)
                dve.wait_ge(mix_done, d + 1)
                dve.wait_ge(gates_sig, d + 1)
                for f in range(2):
                    v = sg[:, f, :].rearrange("p (a n) -> p a n", a=2)
                    last = dve.tensor_tensor(v, v, ps[:, 4 + 2 * f:6 + 2 * f, 0:HALF_NT], ALU.mult)
                last.then_inc(mix_used, 1)
                dve.wait_ge(mix_used, d + 1)
                if d >= 1:
                    dve.wait_ge(m_lo, d)
                dve.tensor_tensor(sg[:, 2, :], sg[:, 0, :], sg[:, 1, :], ALU.add).then_inc(mixed, 1)
                dve.wait_ge(m_hi, d + 1)
                dve.tensor_tensor(mlo[:, d, :], sg[:, 2, :], mhi[:, d, :].bitcast(F32), ALU.subtract).then_inc(m_lo, 1)
                w_low(N_PROJ + 2 * d + 3)

            dve.wait_ge(res_in, 32)
            for g in range(20):
                o, t = divmod(g, 5)
                n = TILES[t][1]
                dve.wait_ge(y_done, g + 1)
                v = res[0:n, t, UC * o:UC * o + UC]
                ins = dve.tensor_tensor(v, v, ps[0:n, g % 8, 0:UC], ALU.add)
                if t == 4:
                    dve.wait_ge(y_low, o + 1)
                    link(ins)
                    ins = dve.tensor_tensor(v, v, low_part[0:DEC, :], ALU.add)
                ins.then_inc(y_out, 1)
                if t == 4 and o + 2 < D // UC:
                    w_low(N_PROJ + 2 * (D // P) + o + 2)

        @block.gpsimd
        def _(pool):
            chain = [0]

            def link(ins):
                chain[0] += 1
                ins.then_inc(pool_chain, 1)
                pool.wait_ge(pool_chain, chain[0])

            pool.memset(ident, 0.0).then_inc(const_ready, 1)
            pool.memset(tri_f, -1.0).then_inc(const_ready, 1)
            pool.memset(ones_f, -1.0).then_inc(const_ready, 1)
            pool.memset(halves, -0.5)
            pool.wait_ge(const_ready, 3)
            pool.affine_select(ident, ident, [[-1, P]], ALU.not_equal, 1.0, base=0, channel_multiplier=1).then_inc(const_ready, 1)

            def inverse_root(out, sums, n, width, cols):
                link(pool.tensor_scalar(sums, sums, 1.0 / n, EPS, ALU.mult, ALU.add))
                return pool.tensor_tensor(out, sums, halves[0:sums.shape[0], 0:cols] if width is None else width, ALU.pow)

            for t, (t0, n) in enumerate(TILES):
                pool.wait_ge(x_sq, t + 1)
                inverse_root(xrs[0:n, t:t + 1], xss[0:n, t:t + 1], D, None, 1).then_inc(x_rs, 1)
            for t, (t0, n) in enumerate(TILES):
                if t in (0, 2):
                    pool.wait_ge(x_hi, t + 1)
                    src = wk[:, XSLOT[t], 0:KC * n].rearrange("p (c n) -> p c n", c=KC)
                    pool.tensor_tensor(xlo[:, :, t0:t0 + n], src, xhi[:, :, t0:t0 + n].bitcast(F32),
                                       ALU.subtract).then_inc(x_lo_pool, 1)
            pool.wait_ge(x_lo, 3)
            pool.tensor_copy(xst[:, :, 0:DEC], xhi[:, :, SEQ:NT].bitcast(F32))
            pool.tensor_copy(xst[:, :, DEC:2 * DEC], xlo[:, :, SEQ:NT].bitcast(F32)).then_inc(x_st, 1)
            pool.affine_select(tri_f, tri_f, [[-1, P]], ALU.is_ge, 0.0, base=0, channel_multiplier=1).then_inc(const_ready, 1)
            pool.wait_ge(const_ready, 5)
            link(pool.tensor_copy(tri, tri_f))
            link(pool.tensor_copy(ones, ones_f))
            link(pool.tensor_copy(ident_b, ident))
            link(pool.memset(later, NEG))
            link(pool.affine_select(later, later, [[-1, P]], ALU.is_ge, 0.0, base=0, channel_multiplier=1))
            for q in (qT, qS):
                link(pool.memset(q[HD:P, 0:H:2, :], 0.0))
                link(pool.memset(q[0:HD, 1:H:2, :], 0.0))
            pool.wait_ge(const_in, 64)
            pool.tensor_scalar(gk[:, 0, :], gk[:, 0, :], HD ** -0.5, 0.0, ALU.mult, ALU.add).then_inc(const_ready, 1)

            def add_sample(name):
                pool.wait_ge(group_out, LAST_GROUP[U[name]] + 1)
                c = UC * int(name[2])
                if name[0] == "v":
                    dst = vals[0:DEC, 6, c:c + UC]
                else:
                    c += W if name[:2] == "ka" else 0
                    dst = tm[0:DEC, 4, c:c + UC]
                pool.tensor_tensor(dst, dst, low_part[0:DEC, :], ALU.add).then_inc(sample_rows, 1)

            add_sample("qi0")
            pool.wait_ge(ki_ss, 1)
            link(inverse_root(nrs[:, 0:4, 0], nss[:, 0:4, 0], HD, None, 4))
            inverse_root(nrs[0:DEC, 4:5, 0], nss[0:DEC, 4:5, 0], HD, None, 1).then_inc(ki_rs, 1)
            for name in ("qi1", "vb0", "vb1", "kb0", "kb1"):
                add_sample(name)

            def norm_root(ss, half, rs):
                pool.wait_ge(ss, half + 1)
                for n, t0, t1 in ((P, 0, 4), (DEC, 4, 5)):
                    sums, out = (v[0:n, t0:t1, 4 * half:4 * half + 4] for v in (nss, nrs))
                    exponent = halves[0:n, 0:4 * (t1 - t0)].rearrange("p (t h) -> p t h", h=4)
                    link(pool.tensor_scalar(sums, sums, 1.0 / HD, EPS, ALU.mult, ALU.add))
                    last = pool.tensor_tensor(out, sums, exponent, ALU.pow)
                    if n == P:
                        link(last)
                last.then_inc(rs, 1)

            def spans(s):
                return [(P, 0, PACK)] if s < H else [(P, 0, 512), (DEC, 512, 256)]

            def split(s):
                pool.wait_ge(lh_done, s + 1)
                for n, c, w in spans(s):
                    last = pool.tensor_tensor(Llo[0:n, c:c + w], wk[0:n, 1, c:c + w], Lhi[0:n, c:c + w].bitcast(F32),
                                              ALU.subtract)
                last.then_inc(lm_done, 1)

            g = FIRST_GROUP[U["ka0"]]
            for s in range(10):
                for _ in range(2):
                    if g <= LAST_GROUP[U["qa1"]]:
                        if g == LAST_GROUP[GROUPS[g][0]]:
                            add_sample(UNITS[GROUPS[g][0]][0])
                        g += 1
                if s < 9:
                    split(s)
                if s in (5, 6):
                    norm_root(nk_ss, s - 5, nk_rs)
            norm_root(nq_ss, 0, nq_rs)
            norm_root(nq_ss, 1, nq_rs)
            add_sample("va0")
            add_sample("va1")

            pool.wait_ge(group_out, len(GROUPS))
            pool.wait_ge(pv_out, 5)
            for k in range(4):
                c = (4, 6, 0, 2)[k]
                if k == 2:
                    pool.wait_ge(av_out, 5)
                pool.tensor_tensor(oT[:, c:c + 2, :], oT[:, c:c + 2, :], u[:, c:c + 2, :], ALU.mult).then_inc(ou_done, 1)

            pool.wait_ge(group_done, len(GROUPS))
            pool.wait_ge(m_lo, D // P)
            pool.tensor_copy(xst[:, :, 0:DEC], mhi[:, :, SEQ:NT].bitcast(F32))
            pool.tensor_copy(xst[:, :, DEC:2 * DEC], mlo[:, :, SEQ:NT].bitcast(F32)).then_inc(m_st, 1)


_INS = ["x_prompt", "x_sample", "cache_a_k", "cache_a_v", "cache_idx_k", "cache_b_k", "cache_b_v", "norm_g", "w_in",
        "q_norm_g", "k_norm_g", "idx_k_norm_g", "w_a_out", "w_b_out", "w_o", "rope_const"]
_OUTS = [(1, SEQ, D), (1, DEC, D),
         (1, 1, SEQ, H, HD), (1, 1, SEQ, H, HD), (1, 1, SEQ, HD), (1, 1, SEQ, H, HD), (1, 1, SEQ, H, HD),
         (1, 1, DEC, H, HD), (1, 1, DEC, H, HD), (1, 1, DEC, HD), (1, 1, DEC, H, HD), (1, 1, DEC, H, HD)]


def rope_tables():
    half = HR
    freq = np.float32(500000.0) ** (-np.arange(half, dtype=np.float32) / np.float32(half))
    pos = np.zeros((5, P), np.float32)
    pos[0:4] = np.arange(SEQ, dtype=np.float32).reshape(4, P)
    pos[4, 0:DEC] = PAST + np.arange(DEC, dtype=np.float32)
    ang = pos[:, :, None] * freq[None, None, :].astype(np.float32)
    cos, sin = np.cos(ang), np.sin(ang)
    table = np.concatenate([cos, cos, -sin, sin], axis=-1).astype(np.float32)
    return np.ascontiguousarray(table.transpose(1, 0, 2))


def kernel(**inputs):
    import concourse.bacc as _bacc
    from concourse.bass_utils import run_bass_kernel_spmd as _run

    nc = _bacc.Bacc("TRN2", target_bir_lowering=False, num_devices=1)
    arrays, args = {}, []
    for name in _INS:
        if name == "rope_const":
            a = rope_tables()
        else:
            a = np.ascontiguousarray(inputs[name])
            if name == "norm_g":
                a = np.ascontiguousarray(a.reshape(KC, P).T)
            if name in ("q_norm_g", "k_norm_g", "idx_k_norm_g"):
                a = np.ascontiguousarray(np.broadcast_to(a, (P, HD)))
        arrays[f"in_{name}"] = a
        args.append(nc.dram_tensor(f"in_{name}", a.shape, mybir.dt.from_np(a.dtype), kind="ExternalInput").ap())
    for i, shape in enumerate(_OUTS):
        args.append(nc.dram_tensor(f"out_{i}", shape, F32, kind="ExternalOutput").ap())
    build(nc, *args)
    r = _run(nc, [arrays], core_ids=[0])
    return tuple(r.results[0][f"out_{i}"] for i in range(len(_OUTS)))
```
